# Optimizing a Trainium2 kernel written in Bass

```python
import jax, jax.numpy as jnp
from jax import lax
import numpy as np

D_MODEL = 1024
BATCH = 1
SEQ = 256
DEPTH = 2

HEAD_DIM = 64
ROT_DIM = HEAD_DIM // 4
ROPE_THETA = 500000.0
NORM_EPS = 1e-6
NEG = -1e30
Q_BLOCK = 128

A_HEADS = 8
MOBA_BLOCK = 256
MOBA_TOPK = 3
B_HEADS = 8
IDX_HEADS = 4
IDX_DIM = 64
DSA_TOPK = 256
C_HEADS = 16
DILATED_PAIRS = ((128, 1), (512, 4), (2048, 16))
PEER_HEADS = 8
N_KEYS = 128
N_EXPERTS = N_KEYS * N_KEYS
PEER_TOPK = 16
PEER_QDIM = 256
PEER_TOKEN_BLOCK = 128
PLE_DIM = 256

N_EVEN = (DEPTH + 1) // 2
N_ODD = DEPTH // 2
A_WIDTH = A_HEADS * HEAD_DIM
B_WIDTH = B_HEADS * HEAD_DIM
AB_WIDTH = A_WIDTH + B_WIDTH
AB_IN = 3 * AB_WIDTH + IDX_HEADS * IDX_DIM + IDX_DIM + IDX_HEADS
C_WIDTH = C_HEADS * HEAD_DIM
C_IN = 3 * C_WIDTH

kernel_name = "hybrid_moba_dsa_dilated_peer_trunk"

def rmsnorm(x, g):
    xf = x.astype(jnp.float32)
    y = xf * lax.rsqrt(jnp.mean(xf * xf, axis=-1, keepdims=True) + NORM_EPS)
    return (y * g.astype(jnp.float32)).astype(x.dtype)

def rope_tables(positions):
    half = ROT_DIM // 2
    inv = ROPE_THETA ** (-jnp.arange(half, dtype=jnp.float32) / half)
    ang = positions.astype(jnp.float32)[..., None] * inv
    return jnp.cos(ang)[:, :, None, :], jnp.sin(ang)[:, :, None, :]

def partial_rope(x, cos, sin):
    half = ROT_DIM // 2
    xf = x.astype(jnp.float32)
    x1 = xf[..., :half]
    x2 = xf[..., half:ROT_DIM]
    out = jnp.concatenate([x1 * cos - x2 * sin, x2 * cos + x1 * sin, xf[..., ROT_DIM:]], axis=-1)
    return out.astype(x.dtype)

def qk_prep(q, k, gq, gk, cos, sin):
    return partial_rope(rmsnorm(q, gq), cos, sin), partial_rope(rmsnorm(k, gk), cos, sin)

def moba_attention(q, k, v):
    B, S, H, dh = q.shape
    scale = dh ** -0.5
    Sp = -(-S // MOBA_BLOCK) * MOBA_BLOCK
    pad = ((0, 0), (0, Sp - S), (0, 0), (0, 0))
    qp, kp, vp = [jnp.pad(a, pad).transpose(0, 2, 1, 3) for a in (q, k, v)]
    nb = Sp // MOBA_BLOCK
    qb = qp.reshape(B, H, nb, MOBA_BLOCK, dh)
    kb = kp.reshape(B, H, nb, MOBA_BLOCK, dh)
    vb = vp.reshape(B, H, nb, MOBA_BLOCK, dh)
    s_own = jnp.einsum('bhnqd,bhnkd->bhnqk', qb, kb).astype(jnp.float32) * scale
    causal = jnp.tril(jnp.ones((MOBA_BLOCK, MOBA_BLOCK), dtype=bool))
    s_own = jnp.where(causal, s_own, NEG)
    m_own = jnp.max(s_own, axis=-1)
    p_own = jnp.exp(s_own - m_own[..., None])
    l_own = jnp.sum(p_own, axis=-1)
    o_own = jnp.einsum('bhnqk,bhnkd->bhnqd', p_own, vb.astype(jnp.float32)) / l_own[..., None]
    o_own = o_own.reshape(B, H, Sp, dh)
    lse_own = (m_own + jnp.log(l_own)).reshape(B, H, Sp)
    n_sel = min(MOBA_TOPK, nb - 1)
    if n_sel == 0:
        out = o_own
    else:
        kmean = jnp.mean(kb.astype(jnp.float32), axis=3)
        gate = jnp.einsum('bhsd,bhnd->bhsn', qp.astype(jnp.float32), kmean)
        qblk = jnp.arange(Sp) // MOBA_BLOCK
        past = jnp.arange(nb)[None, :] < qblk[:, None]
        gate = jnp.where(past, gate, NEG)
        _, gidx = lax.top_k(gate, n_sel)
        gvalid = gidx < qblk[:, None]
        nq = Sp // Q_BLOCK
        to_chunks = lambda a: jnp.moveaxis(a.reshape(B, H, nq, Q_BLOCK, *a.shape[3:]), 2, 0)
        bi = jnp.arange(B)[:, None, None, None]
        hi = jnp.arange(H)[None, :, None, None]

        def sel_step(args):
            qc, ic, vc = args
            kg = kb[bi, hi, ic]
            vg = vb[bi, hi, ic]
            s = jnp.einsum('bhqd,bhqnkd->bhqnk', qc, kg).astype(jnp.float32) * scale
            s = jnp.where(vc[..., None], s, NEG).reshape(B, H, Q_BLOCK, n_sel * MOBA_BLOCK)
            m = jnp.max(s, axis=-1)
            pr = jnp.exp(s - m[..., None])
            l = jnp.sum(pr, axis=-1)
            o = jnp.einsum('bhqj,bhqjd->bhqd', pr,
                           vg.reshape(B, H, Q_BLOCK, n_sel * MOBA_BLOCK, dh).astype(jnp.float32)) / l[..., None]
            return o, m + jnp.log(l)

        o_sel, lse_sel = lax.map(sel_step, (to_chunks(qp), to_chunks(gidx), to_chunks(gvalid)))
        o_sel = jnp.moveaxis(o_sel, 0, 2).reshape(B, H, Sp, dh)
        lse_sel = jnp.moveaxis(lse_sel, 0, 2).reshape(B, H, Sp)
        mx = jnp.maximum(lse_own, lse_sel)
        w1 = jnp.exp(lse_own - mx)
        w2 = jnp.exp(lse_sel - mx)
        out = (o_own * w1[..., None] + o_sel * w2[..., None]) / (w1 + w2)[..., None]
    return out.transpose(0, 2, 1, 3)[:, :S].astype(q.dtype)

def dsa_attention(q, k, v, q_idx, k_idx, w_idx):
    B, S, H, dh = q.shape
    n_sel = min(DSA_TOPK, S // 4)
    nq = S // Q_BLOCK
    scale = dh ** -0.5
    kpos = jnp.arange(S)
    bi = jnp.arange(B)[:, None, None]
    to_chunks = lambda a: jnp.moveaxis(a.reshape(B, nq, Q_BLOCK, *a.shape[2:]), 1, 0)

    def step(args):
        qc, qic, wc, t0 = args
        tpos = t0 + jnp.arange(Q_BLOCK)
        logits = jnp.einsum('bqhd,bsd->bqhs', qic, k_idx).astype(jnp.float32)
        score = jnp.einsum('bqh,bqhs->bqs', wc.astype(jnp.float32), jax.nn.relu(logits))
        adm = kpos[None, :] <= tpos[:, None]
        score = jnp.where(adm, score, NEG)
        _, sidx = lax.top_k(score, n_sel)
        valid = sidx <= tpos[None, :, None]
        kg = k[bi, sidx]
        vg = v[bi, sidx]
        s = jnp.einsum('bqhd,bqnhd->bqhn', qc, kg).astype(jnp.float32) * scale
        s = jnp.where(valid[:, :, None, :], s, NEG)
        pr = jax.nn.softmax(s, axis=-1)
        return jnp.einsum('bqhn,bqnhd->bqhd', pr, vg.astype(jnp.float32)).astype(q.dtype)

    t0s = jnp.arange(nq, dtype=jnp.int32) * Q_BLOCK
    o = lax.map(step, (to_chunks(q), to_chunks(q_idx), to_chunks(w_idx), t0s))
    return jnp.moveaxis(o, 0, 1).reshape(B, S, H, dh)

def dilated_branch(q, k, v, window, dil):
    B, S, H, dh = q.shape
    band = window // dil
    scale = dh ** -0.5
    span = dil * band
    Sp = -(-S // span) * span
    M = Sp // dil
    nb = M // band

    def split(a):
        a = jnp.pad(a, ((0, 0), (0, Sp - S), (0, 0), (0, 0)))
        a = a.reshape(B, M, dil, H, dh).transpose(0, 2, 3, 1, 4)
        return a.reshape(B, dil, H, nb, band, dh)

    def with_prev(a):
        prev = jnp.pad(a, ((0, 0), (0, 0), (0, 0), (1, 0), (0, 0), (0, 0)))[:, :, :, :-1]
        return jnp.concatenate([prev, a], axis=4)

    qb = split(q)
    kk = with_prev(split(k))
    vv = with_prev(split(v))
    s = jnp.einsum('brhnqd,brhnkd->brhnqk', qb, kk).astype(jnp.float32) * scale
    i = jnp.arange(band)[:, None]
    j = jnp.arange(2 * band)[None, :]
    dist = i + band - j
    in_band = (dist >= 0) & (dist <= band)
    mask = in_band[None] & ((jnp.arange(nb)[:, None, None] > 0) | (j[None] >= band))
    s = jnp.where(mask, s, NEG)
    m = jnp.max(s, axis=-1)
    pr = jnp.exp(s - m[..., None])
    l = jnp.sum(pr, axis=-1)
    o = jnp.einsum('brhnqk,brhnkd->brhnqd', pr, vv.astype(jnp.float32)) / l[..., None]
    lse = m + jnp.log(l)
    o = o.reshape(B, dil, H, M, dh).transpose(0, 3, 1, 2, 4).reshape(B, Sp, H, dh)[:, :S]
    lse = lse.reshape(B, dil, H, M).transpose(0, 3, 1, 2).reshape(B, Sp, H)[:, :S]
    return o, lse

def dilated_attention(q, k, v):
    outs, lses = [], []
    for window, dil in DILATED_PAIRS:
        o, lse = dilated_branch(q, k, v, window, dil)
        outs.append(o)
        lses.append(lse)
    wts = jax.nn.softmax(jnp.stack(lses, axis=0), axis=0)
    return jnp.einsum('gbsh,gbshd->bshd', wts, jnp.stack(outs, axis=0)).astype(q.dtype)

def ab_mixer(xn, cos, sin, w_in, w_out, a_q_norm, a_k_norm, b_q_norm, b_k_norm):
    B, S, _ = xn.shape
    sizes = [A_WIDTH, A_WIDTH, A_WIDTH, B_WIDTH, B_WIDTH, B_WIDTH, IDX_HEADS * IDX_DIM, IDX_DIM, IDX_HEADS]
    cuts = np.cumsum(sizes)[:-1].tolist()
    qa, ka, va, qb, kb, vb, qi, ki, wi = jnp.split(xn @ w_in, cuts, axis=-1)
    heads = lambda a, n: a.reshape(B, S, n, -1)
    qa, ka = qk_prep(heads(qa, A_HEADS), heads(ka, A_HEADS), a_q_norm, a_k_norm, cos, sin)
    oa = moba_attention(qa, ka, heads(va, A_HEADS))
    qb, kb = qk_prep(heads(qb, B_HEADS), heads(kb, B_HEADS), b_q_norm, b_k_norm, cos, sin)
    qi = partial_rope(heads(qi, IDX_HEADS), cos, sin)
    ki = partial_rope(ki[:, :, None, :], cos, sin)[:, :, 0]
    ob = dsa_attention(qb, kb, heads(vb, B_HEADS), qi, ki, wi)
    o = jnp.concatenate([oa.reshape(B, S, A_WIDTH), ob.reshape(B, S, B_WIDTH)], axis=-1)
    return o @ w_out

def c_mixer(xn, cos, sin, w_in, w_out, q_norm, k_norm):
    B, S, _ = xn.shape
    q, k, v = jnp.split(xn @ w_in, 3, axis=-1)
    heads = lambda a: a.reshape(B, S, C_HEADS, HEAD_DIM)
    q, k = qk_prep(heads(q), heads(k), q_norm, k_norm, cos, sin)
    o = dilated_attention(q, k, heads(v))
    return o.reshape(B, S, C_WIDTH) @ w_out

def peer_ffn(xn, w_query, sub_keys, expert_u, expert_v):
    B, S, D = xn.shape
    T = B * S
    xt = xn.reshape(T // PEER_TOKEN_BLOCK, PEER_TOKEN_BLOCK, D)

    def step(xc):
        tc = xc.shape[0]
        qry = (xc @ w_query).reshape(tc, PEER_HEADS, 2, PEER_QDIM // 2)
        s = jnp.einsum('thcd,hckd->thck', qry, sub_keys).astype(jnp.float32)
        sv, si = lax.top_k(s, PEER_TOPK)
        cand = (sv[:, :, 0, :, None] + sv[:, :, 1, None, :]).reshape(tc, PEER_HEADS, PEER_TOPK * PEER_TOPK)
        cidx = (si[:, :, 0, :, None] * N_KEYS + si[:, :, 1, None, :]).reshape(tc, PEER_HEADS, PEER_TOPK * PEER_TOPK)
        cv, ci = lax.top_k(cand, PEER_TOPK)
        eidx = jnp.take_along_axis(cidx, ci, axis=-1)
        g = jax.nn.softmax(cv, axis=-1)
        u = expert_u[eidx]
        a = jax.nn.gelu(jnp.einsum('td,thkd->thk', xc, u).astype(jnp.float32))
        ve = expert_v[eidx]
        return jnp.einsum('thk,thkd->td', (g * a).astype(ve.dtype), ve).astype(xc.dtype)

    return lax.map(step, xt).reshape(B, S, D)

def setup_inputs(seed: int = 0) -> dict:
    key = jax.random.key(seed)
    ks = jax.random.split(key, 24)
    f32 = jnp.float32
    nrm = lambda k, shape, sc: jax.random.normal(k, shape, f32) * sc
    gain = lambda k, shape: 1.0 + 0.05 * jax.random.normal(k, shape, f32)
    return {
        "x": nrm(ks[0], (BATCH, SEQ, D_MODEL), 1.0),
        "p": nrm(ks[1], (DEPTH, BATCH, SEQ, PLE_DIM), 1.0),
        "positions": jnp.broadcast_to(jnp.arange(SEQ, dtype=jnp.int32), (BATCH, SEQ)),
        "attn_norm": gain(ks[2], (DEPTH, D_MODEL)),
        "ffn_norm": gain(ks[3], (DEPTH, D_MODEL)),
        "ple_norm": gain(ks[4], (DEPTH, D_MODEL)),
        "ab_w_in": nrm(ks[5], (N_EVEN, D_MODEL, AB_IN), D_MODEL ** -0.5),
        "ab_w_out": nrm(ks[6], (N_EVEN, AB_WIDTH, D_MODEL), AB_WIDTH ** -0.5),
        "a_q_norm": gain(ks[7], (N_EVEN, HEAD_DIM)),
        "a_k_norm": gain(ks[8], (N_EVEN, HEAD_DIM)),
        "b_q_norm": gain(ks[9], (N_EVEN, HEAD_DIM)),
        "b_k_norm": gain(ks[10], (N_EVEN, HEAD_DIM)),
        "c_w_in": nrm(ks[11], (N_ODD, D_MODEL, C_IN), D_MODEL ** -0.5),
        "c_w_out": nrm(ks[12], (N_ODD, C_WIDTH, D_MODEL), C_WIDTH ** -0.5),
        "c_q_norm": gain(ks[13], (N_ODD, HEAD_DIM)),
        "c_k_norm": gain(ks[14], (N_ODD, HEAD_DIM)),
        "peer_w_query": nrm(ks[15], (DEPTH, D_MODEL, PEER_HEADS * PEER_QDIM), D_MODEL ** -0.5),
        "peer_sub_keys": nrm(ks[16], (DEPTH, PEER_HEADS, 2, N_KEYS, PEER_QDIM // 2), (PEER_QDIM // 2) ** -0.5),
        "peer_u": nrm(ks[17], (DEPTH, N_EXPERTS, D_MODEL), D_MODEL ** -0.5),
        "peer_v": nrm(ks[18], (DEPTH, N_EXPERTS, D_MODEL), PEER_HEADS ** -0.5),
        "ple_w_gate": nrm(ks[19], (DEPTH, D_MODEL, D_MODEL), D_MODEL ** -0.5),
        "ple_w_up": nrm(ks[20], (DEPTH, PLE_DIM, D_MODEL), PLE_DIM ** -0.5),
    }

def reference(x, p, positions, attn_norm, ffn_norm, ple_norm, ab_w_in, ab_w_out,
              a_q_norm, a_k_norm, b_q_norm, b_k_norm, c_w_in, c_w_out, c_q_norm, c_k_norm,
              peer_w_query, peer_sub_keys, peer_u, peer_v, ple_w_gate, ple_w_up):
    cos, sin = rope_tables(positions)
    h = x
    for i in range(DEPTH):
        xn = rmsnorm(h, attn_norm[i])
        if i % 2 == 0:
            j = i // 2
            h = h + ab_mixer(xn, cos, sin, ab_w_in[j], ab_w_out[j],
                             a_q_norm[j], a_k_norm[j], b_q_norm[j], b_k_norm[j])
        else:
            j = i // 2
            h = h + c_mixer(xn, cos, sin, c_w_in[j], c_w_out[j], c_q_norm[j], c_k_norm[j])
        h = h + peer_ffn(rmsnorm(h, ffn_norm[i]), peer_w_query[i], peer_sub_keys[i], peer_u[i], peer_v[i])
        gate = jax.nn.sigmoid(rmsnorm(h, ple_norm[i]) @ ple_w_gate[i])
        h = h + (p[i] @ ple_w_up[i]) * gate
    return h


_drawn_inputs = setup_inputs


def setup_inputs(seed=0):
    import zlib

    import numpy as np

    out = dict(_drawn_inputs(seed))
    spreads = {}
    factors = {'ple_norm': 3.183,
     'a_q_norm': 2.723,
     'a_k_norm': 2.821,
     'c_q_norm': 4.033,
     'c_k_norm': 4.014}
    for name, (base, spread) in spreads.items():
        noise = np.random.default_rng([zlib.crc32(name.encode()), seed]).standard_normal(out[name].shape)
        drawn = base * np.exp(spread * noise) if base else spread * noise
        out[name] = __import__('jax').numpy.asarray(drawn.astype(out[name].dtype))
    for name, factor in factors.items():
        out[name] = (out[name] * factor).astype(out[name].dtype)
    return out
```

```python
from contextlib import ExitStack

import numpy as np

import concourse.bass as bass
from concourse import mybir

ALU = mybir.AluOpType
ACT = mybir.ActivationFunctionType
F32 = mybir.dt.float32
U32 = mybir.dt.uint32
I32 = mybir.dt.int32
AX_X = mybir.AxisListType.X

P = 128
D = 1024
S = 256
NT = S // P
NC = D // P
LAYERS = 2
DH = 64
ROT = 16
HALF = ROT // 2
EPS = 1e-6
NEG = -1e30
GONE = -3e38
HEADS = 16
PAIRS = HEADS // 2
IN_WIDTH = (3396, 3072)
V_COL = ([1024 + DH * h for h in range(8)] + [2560 + DH * h for h in range(8)],
         [2048 + DH * h for h in range(16)])
QK_RUN = ((0, 1536), (0, 1024))
Q_COL = ([128 * p for p in range(4)] + [1536 + 128 * p for p in range(4)], [128 * p for p in range(8)])
K_COL = ([512 + 128 * p for p in range(4)] + [2048 + 128 * p for p in range(4)],
         [1024 + 128 * p for p in range(8)])
IDX_COL, IDX_HEADS, WI_COL = 3072, 4, 3392
DSA_TOPK = 64
PH = 8
HC = 2 * PH
NK = 128
TOPK = 16
KEYS = P + 2 * P
SEG = ((0, P), (P, 3 * P))
SCALE = DH ** -0.5
TWO_PI_PARTS = (6.28125, 1.9350051879882812e-03, 3.0199159819567529e-07)
ROUND = 12582912.0

BLOCKS = []
for _l in range(LAYERS):
    _w = IN_WIDTH[_l]
    BLOCKS += [("in", _l, b, NC, min(512, _w - 512 * b)) for b in range(-(-_w // 512))]
    BLOCKS += [("out", _l, b, NC, 512) for b in range(2)]
    BLOCKS += [("query", _l, b, NC, 512) for b in range(4)]
    BLOCKS += [("gate", _l, b, NC, 512) for b in range(2)]
    BLOCKS += [("up", _l, b, 2, 512) for b in range(2)]
BY_ACT = ("in", "query", "gate")


def blocks_of(kind, l):
    return [n for n, b in enumerate(BLOCKS) if b[0] == kind and b[1] == l]


def act_evacs(n):
    return 2 * sum(1 for b in BLOCKS[:n + 1] if b[0] in BY_ACT)


def hybrid_trunk(nc, a, out):
    with ExitStack() as ctx:
        def sb(name, shape, dt=F32):
            return ctx.enter_context(nc.sbuf_tensor(name, shape, dt))

        def sem(name):
            return ctx.enter_context(nc.semaphore(name))

        h = sb("h", [P, NT, D])
        xnT = sb("xnT", [P, NC, S])
        arena = sb("arena", [P, P * S])
        wring = sb("wring", [P, 2, NC * 512])
        uring = sb("uring", [P, 2, NC * P])
        vring = sb("vring", [P, 2, D])
        wbuf = sb("wbuf", [P, 2, S])
        ident = sb("ident", [P, P])
        iota = sb("iota", [P, P])
        bias_causal = sb("bias_causal", [P, KEYS])
        bias_dilated = sb("bias_dilated", [P, KEYS])
        gain = sb("gain", [P, 3 * LAYERS * NC])
        head_gain = sb("head_gain", [P, LAYERS, 2, 2, DH])
        inv_freq = sb("inv_freq", [P, HALF])
        pos_i = sb("pos_i", [P, NT], I32)
        pos_f = sb("pos_f", [P, NT])
        rope_a = sb("rope_a", [P, 4, NT, HALF])
        rope_cos = sb("rope_cos", [P, NT, ROT])
        rope_sin = sb("rope_sin", [P, NT, ROT])
        sumsq = sb("sumsq", [P, NT])
        inv_var = sb("inv_var", [P, NT])
        rstd = sb("rstd", [P, NT])
        h_sumsq = sb("h_sumsq", [P, 2 * NT, HEADS])
        h_inv_var = sb("h_inv_var", [P, 2 * NT, HEADS])
        h_rstd = sb("h_rstd", [P, 2 * NT, HEADS])
        top8 = sb("top8", [P, 8])
        neg_max = sb("neg_max", [P, 2, NT])
        denom = sb("denom", [P, 2, NT])
        inv_denom = sb("inv_denom", [P, 2, NT])
        cv = sb("cv", [P, NT, PH, TOPK])
        e_g = sb("e_g", [P, NT, PH, TOPK])
        g_sum = sb("g_sum", [P, NT, PH])
        g_inv = sb("g_inv", [P, NT, PH])
        ijgT = sb("ijgT", [P, 3, S])

        at = [0]

        def region(n):
            at[0] += n
            return arena[:, at[0] - n:at[0]]

        xs = region(NT * D).rearrange("p (t d) -> p t d", t=NT)
        qkv = region(NT * IN_WIDTH[0]).rearrange("p (t n) -> p t n", t=NT)
        qkT = region(PAIRS * 2 * S).rearrange("p (a k t) -> p a k t", a=PAIRS, k=2)
        oT = region(PAIRS * S).rearrange("p (a t) -> p a t", a=PAIRS)
        early = region(2 * NT * HEADS * DH)
        qryT = early.rearrange("p (a t) -> p a t", a=HC)
        squares = early.rearrange("p (u n d) -> p u n d", u=2 * NT, d=DH)
        rope_t = region(2 * HEADS * ROT).rearrange("p (b n r) -> p b n r", b=2, r=ROT)
        kk = region(NT * P).rearrange("p (t n) -> p t n", t=NT)
        idxT = region(3 * S).rearrange("p (a t) -> p a t", a=3)
        idx_s = region(KEYS)
        idx_r = region(KEYS)
        bias_dsa = region(KEYS)
        biased = region(2 * KEYS).rearrange("p (b n) -> p b n", b=2)
        probs = region(2 * KEYS).rearrange("p (b n) -> p b n", b=2)
        probs_n = region(2 * KEYS).rearrange("p (b n) -> p b n", b=2)
        probs_T = region(2 * KEYS).rearrange("p (b n) -> p b n", b=2)
        sig = region(NT * D).rearrange("p (t d) -> p t d", t=NT)
        keysT = region(HC * NK).rearrange("p (a k) -> p a k", a=HC)
        assert at[0] <= P * S
        act_ijt = arena[:, :].rearrange("p (j t) -> p j t", t=S)
        act_itj = arena[:, :].rearrange("p (j t) -> p t j", t=S)

        flat = wring[:, :, :].rearrange("p b n -> p (b n)")
        sel_at = [0]

        def sel(n, *shape, dt=F32):
            sel_at[0] += n
            v = flat[:, sel_at[0] - n:sel_at[0]]
            v = v if dt is F32 else v.bitcast(dt)
            names = "abcd"[:len(shape)]
            sizes = dict(zip(names, shape))
            return v.rearrange(f"p ({' '.join(names)}) -> p {' '.join(names)}", **sizes)

        key_s = sel(HC * NK, HC, NK)
        cand = sel(PH * TOPK * TOPK, PH, TOPK, TOPK)
        eq = sel(PH * TOPK * TOPK, PH, TOPK, TOPK)
        sv = sel(HC * TOPK, HC, TOPK)
        si = sel(HC * TOPK, HC, TOPK, dt=U32)
        si_f = sel(HC * TOPK, HC, TOPK)
        ci = sel(PH * TOPK, PH, TOPK, dt=U32)
        rank = sel(2 * PH * TOPK, 2, PH, TOPK, dt=U32)
        rank_f = sel(2 * PH * TOPK, 2, PH, TOPK)
        e_i = sel(NT * PH * TOPK, NT, PH, TOPK)
        e_j = sel(NT * PH * TOPK, NT, PH, TOPK)
        assert sel_at[0] <= 2 * NC * 512
        hot_i = flat[:, 0:1024].rearrange("p (b q i) -> p b q i", b=2, q=4)
        hot_j = flat[:, 1024:2048].rearrange("p (b q j) -> p b q j", b=2, q=4)

        bank = [ctx.enter_context(nc.psum_tensor(f"bank{i}", [P, 512], F32)) for i in range(8)]

        const_loaded = sem("const_loaded")
        h_loaded = sem("h_loaded")
        rope_step = sem("rope_step")
        angle_ready = sem("angle_ready")
        rope_ready = sem("rope_ready")
        w_loaded = [sem("w_loaded0"), sem("w_loaded1")]
        keys_loaded = sem("keys_loaded")
        u_loaded = [sem("u_loaded0"), sem("u_loaded1")]
        v_loaded = [sem("v_loaded0"), sem("v_loaded1")]
        stored = sem("stored")
        sumsq_done = sem("sumsq_done")
        var_ready = sem("var_ready")
        rstd_ready = sem("rstd_ready")
        xs_ready = sem("xs_ready")
        xs_turned = sem("xs_turned")
        xnT_by_dve = sem("xnT_by_dve")
        xnT_by_act = sem("xnT_by_act")
        proj_done = sem("proj_done")
        proj_taken = sem("proj_taken")
        h_written = sem("h_written")
        qk_squared = sem("qk_squared")
        h_var_ready = sem("h_var_ready")
        h_rstd_ready = sem("h_rstd_ready")
        qk_ready = sem("qk_ready")
        idx_ready = sem("idx_ready")
        qk_turned = sem("qk_turned")
        qkT_ready = sem("qkT_ready")
        idx_turned = sem("idx_turned")
        idxT_ready = sem("idxT_ready")
        logits_done = sem("logits_done")
        even_logits = sem("even_logits")
        scores_done = sem("scores_done")
        biased_ready = sem("biased_ready")
        negmax_ready = sem("negmax_ready")
        exp_done = sem("exp_done")
        probs_ready = sem("probs_ready")
        probs_turned = sem("probs_turned")
        probsT_ready = sem("probsT_ready")
        pv_done = sem("pv_done")
        oT_ready = sem("oT_ready")
        keys_scored = sem("keys_scored")
        key_s_ready = sem("key_s_ready")
        u_done = sem("u_done")
        gelu_done = sem("gelu_done")
        cand_ready = sem("cand_ready")
        gexp_done = sem("gexp_done")
        sel_ready = sem("sel_ready")
        sel_turned = sem("sel_turned")
        selT_ready = sem("selT_ready")
        hot_i_ready = sem("hot_i_ready")
        hot_j_ready = sem("hot_j_ready")
        gates_done = sem("gates_done")
        gated_done = sem("gated_done")
        w_ready = sem("w_ready")
        v_done = sem("v_done")
        dve_step = sem("dve_step")

        block = ctx.enter_context(nc.Block())
        CONSTS = 8

        @block.sync
        def _(sp):
            for i in range(NT):
                sp.dma_start(h[:, i, :], a["x"][P * i:P * i + P, :]).then_inc(h_loaded, 16)
            for dst, src in ((ident[:], a["ident"]), (iota[:], a["iota"]), (bias_causal[:], a["bias_causal"]),
                             (bias_dilated[:], a["bias_dilated"]), (gain[:], a["gain"]),
                             (inv_freq[:], a["inv_freq"]), (pos_i[:], a["positions"]),
                             (head_gain[:], a["head_gain"])):
                sp.dma_start(dst, src).then_inc(const_loaded, 16)

            def load_block(n):
                kind, l, b, k, w = BLOCKS[n]
                if n >= 2:
                    sp.wait_ge(proj_done, 2 * (n - 1))
                size = k * w + (2 * S if kind == "up" else 0)
                row = size if kind == "up" else k * 512
                src = a[f"{kind}{l}"][:, b * row:b * row + size]
                sp.dma_start(wring[:, n % 2, 0:size], src).then_inc(w_loaded[n % 2], 16)

            for l in range(LAYERS):
                if l:
                    sp.wait_ge(h_written, 12 * l)
                sp.dma_start(keysT, a["keysT"][l]).then_inc(keys_loaded, 16)
                for kind in ("in", "out", "query"):
                    for n in blocks_of(kind, l):
                        load_block(n)
                with sp.Fori(0, NK // 2) as k:
                    for s in range(2):
                        sp.wait_ge(gelu_done, NK * l + k * 2 + s + 1)
                        sp.dma_start(uring[:, s, :], a["uT"][l, bass.ds(k * 2 + s, 1), :, :]
                                     .rearrange("a p n -> (a p) n")).then_inc(u_loaded[s], 16)
                with sp.Fori(0, NK // 2) as k:
                    for s in range(2):
                        sp.wait_ge(v_done, NK * l + k * 2 + s + 1)
                        sp.dma_start(vring[:, s, :], a["v"][l, bass.ds(k * 2 + s, 1), :, :]
                                     .rearrange("a p n -> (a p) n")).then_inc(v_loaded[s], 16)
                for kind in ("gate", "up"):
                    for n in blocks_of(kind, l):
                        load_block(n)
            sp.wait_ge(h_written, 12 * LAYERS)
            for i in range(NT):
                sp.dma_start(out[P * i:P * i + P, :], h[:, i, :]).then_inc(stored, 16)
            sp.wait_ge(stored, 16 * NT)

        @block.tensor
        def _(pe):
            pe.sem_inc(gates_done, 2)
            pe.sem_inc(v_done, 2)
            pe.wait_ge(const_loaded, 16 * CONSTS)

            def turn_normed(n):
                pe.wait_ge(xs_ready, 2 * (n + 1))
                for g in range(4):
                    for c in (2 * g, 2 * g + 1):
                        for t in range(NT):
                            q = (c % 2) * S + t * P
                            mm = pe.transpose(bank[4 + g][:, q:q + P], xs[:, t, c * P:c * P + P], ident[:])
                    mm.then_inc(xs_turned, 1)

            def await_xnT(n):
                pe.wait_ge(xnT_by_dve, 4 * (n + 1))
                pe.wait_ge(xnT_by_act, 4 * (n + 1))

            def project(kind, l, lhsT):
                for n in blocks_of(kind, l):
                    _, _, b, kc, w = BLOCKS[n]
                    pe.wait_ge(w_loaded[n % 2], 16 * (n // 2 + 1))
                    free_banks(n)
                    wb = wring[:, n % 2, 0:kc * w].rearrange("p (c n) -> p c n", c=kc)
                    for t in range(NT):
                        for c in range(kc):
                            mm = pe.matmul(bank[2 * (n % 2) + t][:, 0:w], lhsT(c, t, n % 2), wb[:, c, :],
                                           start=(c == 0), stop=(c == kc - 1))
                        mm.then_inc(proj_done, 1)

            def free_banks(n):
                if n >= 2:
                    kind, l, b, _, _ = BLOCKS[n - 2]
                    if kind in BY_ACT:
                        pe.wait_ge(proj_taken, act_evacs(n - 2))
                    else:
                        pe.wait_ge(h_written, 12 * l + 2 * b + 2 + (8 if kind == "up" else 0))

            def turn_qk(l):
                pe.wait_ge(qk_ready, 4 * (l + 1))
                for p in range(PAIRS):
                    if p >= 2:
                        pe.wait_ge(qkT_ready, PAIRS * l + p - 1)
                    for i, col in enumerate((Q_COL[l][p], K_COL[l][p])):
                        for t in range(NT):
                            q = i * S + t * P
                            mm = pe.transpose(bank[4 + p % 2][:, q:q + P], qkv[:, t, col:col + P], ident[:])
                    mm.then_inc(qk_turned, 1)

            def index_logits():
                pe.wait_ge(idx_ready, NT)
                for t in range(NT):
                    for i in range(3):
                        src = kk[:, t, :] if i == 2 else qkv[:, t, IDX_COL + P * i:IDX_COL + P * i + P]
                        mm = pe.transpose(bank[6 + t][:, P * i:P * i + P], src, ident[:])
                    mm.then_inc(idx_turned, 1)
                pe.wait_ge(idxT_ready, NT)
                pe.wait_ge(qkT_ready, PAIRS)
                for t in range(NT):
                    for i in (0, 2, 1, 3):
                        o = DH * (i % 2)
                        if i == 1:
                            mm.then_inc(even_logits, 1)
                            pe.wait_ge(even_logits, t + 1)
                        dst = bank[6][:, P * i:P * i + P] if t == 0 else bank[4 + i // 2][:, S * (i % 2):S * (i % 2) + S]
                        mm = pe.matmul(dst, idxT[o:o + DH, i // 2, P * t:P * t + P],
                                       idxT[o:o + DH, 2, 0:P * (t + 1)], start=True, stop=True)
                    mm.then_inc(logits_done, 1)

            def heads(l):
                pe.wait_ge(qkT_ready, PAIRS * (l + 1))

                def scores(i):
                    o, p = DH * (i % 2), i // 2
                    if i >= 2:
                        pe.wait_ge(biased_ready, HEADS * l + i - 1)
                    for t in range(NT):
                        mm = pe.matmul(bank[i % 2][:, SEG[t][0]:SEG[t][1]], qkT[o:o + DH, p, 0, P * t:P * t + P],
                                       qkT[o:o + DH, p, 1, 0:P * (t + 1)], start=True, stop=True)
                    mm.then_inc(scores_done, 1)

                def turn(i):
                    pe.wait_ge(probs_ready, 2 * (HEADS * l + i + 1))
                    if i >= 2:
                        pe.wait_ge(probsT_ready, HEADS * l + i - 1)
                    for q in range(3):
                        mm = pe.transpose(bank[2 + i % 2][:, P * q:P * q + P], probs_n[:, i % 2, P * q:P * q + P], ident[:])
                    mm.then_inc(probs_turned, 1)

                def pv(i):
                    o, p, c = DH * (i % 2), i // 2, V_COL[l][i]
                    pe.wait_ge(probsT_ready, HEADS * l + i + 1)
                    if i % 2 == 0 and p >= 1:
                        pe.wait_ge(oT_ready, PAIRS * l + p)
                    for t in range(NT):
                        for s in range(t + 1):
                            q = SEG[t][0] + P * s
                            mm = pe.matmul(bank[7][o:o + DH, P * t:P * t + P],
                                           qkv[:, s, c:c + DH], probs_T[:, i % 2, q:q + P],
                                           start=(s == 0), stop=(s == t))
                    mm.then_inc(pv_done, 1)

                for i in range(HEADS + 2):
                    if i < HEADS:
                        scores(i)
                    if 1 <= i <= HEADS:
                        turn(i - 1)
                    if i >= 2:
                        pv(i - 2)

            def retrieve(l):
                await_xnT(3 * l + 1)
                for n in blocks_of("query", l):
                    pe.wait_ge(w_loaded[n % 2], 16 * (n // 2 + 1))
                    free_banks(n)
                    wb = wring[:, n % 2, :].rearrange("p (c n) -> p c n", c=NC)
                    for part in range(2):
                        for i in range(2):
                            q = P * (2 * part + i)
                            for c in range(NC):
                                mm = pe.matmul(bank[2 * (n % 2) + part][:, S * i:S * i + S], wb[:, c, q:q + P],
                                               xnT[:, c, :], start=(c == 0), stop=(c == NC - 1))
                        mm.then_inc(proj_done, 1)
                pe.wait_ge(proj_taken, act_evacs(blocks_of("query", l)[-1]))
                pe.wait_ge(keys_loaded, 16 * (l + 1))
                for u in range(2 * 4):
                    t, g = u // 4, u % 4
                    for i in range(4):
                        mm = pe.matmul(bank[4 * (1 - t) + g][:, P * i:P * i + P], qryT[:, 4 * g + i, P * t:P * t + P],
                                       keysT[:, 4 * g + i, :], start=True, stop=True)
                    mm.then_inc(keys_scored, 1)
                pe.wait_ge(key_s_ready, 4 * (l + 1))

            def expert_u(l):
                with pe.Fori(0, NK // 2) as k:
                    for s in range(2):
                        pe.wait_ge(u_loaded[s], (k + 1 + l * (NK // 2)) * 16)
                        pe.wait_ge(gelu_done, NK * l + k * 2 + s + 1)
                        for c in range(NC):
                            mm = pe.matmul(bank[4 + s][:, 0:S], uring[:, s, P * c:P * c + P], xnT[:, c, :],
                                           start=(c == 0), stop=(c == NC - 1))
                        mm.then_inc(u_done, 1)

            def gates(l):
                pe.wait_ge(gelu_done, NK * (l + 1) + 2)
                for t in range(NT):
                    pe.wait_ge(sel_ready, 2 * l + t + 1)
                    for i, e in enumerate((e_i, e_j, e_g)):
                        mm = pe.transpose(bank[6 + t][:, P * i:P * i + P], e[:, t, :, :].rearrange("p g k -> p (g k)"), ident[:])
                    mm.then_inc(sel_turned, 1)
                with pe.Fori(0, S // 8) as k:
                    for s in range(2):
                        pe.wait_ge(hot_i_ready, 64 * l + k * 2 + s + 1)
                        pe.wait_ge(hot_j_ready, 64 * l + k * 2 + s + 1)
                        pe.wait_ge(gated_done, 64 * l + k * 2 + s + 1)
                        for q in range(4):
                            mm = pe.matmul(bank[4 + s][:, P * q:P * q + P], hot_i[:, s, q, :], hot_j[:, s, q, :],
                                           start=True, stop=True)
                        mm.then_inc(gates_done, 1)

            def expert_v(l):
                def pair(k, first=False, last=False):
                    for s in range(2):
                        pe.wait_ge(v_loaded[s], (k + 1 + l * (NK // 2)) * 16)
                        pe.wait_ge(w_ready, NK * l + k * 2 + s + 1)
                        for t in range(NT):
                            for b in range(2):
                                mm = pe.matmul(bank[2 * t + b][:, :], wbuf[:, s, P * t:P * t + P],
                                               vring[:, s, 512 * b:512 * b + 512],
                                               start=first and s == 0, stop=last and s == 1)
                        mm.then_inc(v_done, 1)

                pair(0, first=True)
                with pe.Fori(1, NK // 2 - 1) as k:
                    pair(k)
                pair(NK // 2 - 1, last=True)

            for l in range(LAYERS):
                turn_normed(3 * l)
                await_xnT(3 * l)
                project("in", l, lambda c, t, slot: xnT[:, c, P * t:P * t + P])
                turn_qk(l)
                if l == 0:
                    index_logits()
                heads(l)
                pe.wait_ge(oT_ready, PAIRS * (l + 1))
                project("out", l, lambda c, t, slot: oT[:, c, P * t:P * t + P])
                turn_normed(3 * l + 1)
                retrieve(l)
                expert_u(l)
                gates(l)
                expert_v(l)
                turn_normed(3 * l + 2)
                await_xnT(3 * l + 2)
                project("gate", l, lambda c, t, slot: xnT[:, c, P * t:P * t + P])
                project("up", l, lambda c, t, slot: wring[:, slot, 2 * 512 + S * c + P * t:2 * 512 + S * c + P * t + P])

        @block.scalar
        def _(act):
            act.sem_inc(gelu_done, 2)
            act.wait_ge(const_loaded, 16 * CONSTS)
            act.wait_ge(angle_ready, 1)
            act.activation(rope_sin[:, :, HALF:ROT], rope_a[:, 0, :, :], ACT.Sin)
            act.activation(rope_cos[:, :, 0:HALF], rope_a[:, 1, :, :], ACT.Sin).then_inc(rope_ready, 1)

            def norm(n):
                if n:
                    act.wait_ge(h_written, 4 * n)
                else:
                    act.wait_ge(h_loaded, 16 * NT)
                for t in range(NT):
                    act.activation(xs[:, t, :], h[:, t, :], ACT.Square, accum_out=sumsq[:, t:t + 1]).then_inc(sumsq_done, 1)
                act.wait_ge(var_ready, n + 1)
                act.activation(rstd[:], inv_var[:], ACT.Sqrt).then_inc(rstd_ready, 1)
                for c in range(4, 8):
                    act.wait_ge(xs_turned, 4 * n + c // 2 + 1)
                    act.activation(xnT[:, c, :], bank[4 + c // 2][:, S * (c % 2):S * (c % 2) + S], ACT.Copy,
                                   scale=gain[:, n * NC + c:n * NC + c + 1]).then_inc(xnT_by_act, 1)

            def take(kind, l, dst, func):
                for n in blocks_of(kind, l):
                    _, _, b, _, w = BLOCKS[n]
                    for t in range(2):
                        act.wait_ge(proj_done, 2 * n + t + 1)
                        act.activation(dst(b, t, w), bank[2 * (n % 2) + t][:, 0:w], func).then_inc(proj_taken, 1)

            def heads(l):
                def exps(i):
                    act.wait_ge(negmax_ready, 2 * (HEADS * l + i + 1))
                    if i >= 2:
                        act.wait_ge(probs_ready, 2 * (HEADS * l + i - 1))
                    for t, (x, y) in enumerate(SEG):
                        act.activation(probs[:, i % 2, x:y], biased[:, i % 2, x:y], ACT.Exp,
                                       bias=neg_max[:, i % 2, t:t + 1],
                                       accum_out=denom[:, i % 2, t:t + 1]).then_inc(exp_done, 1)

                def take_probs(i):
                    act.wait_ge(probs_turned, HEADS * l + i + 1)
                    if i >= 2:
                        act.wait_ge(pv_done, HEADS * l + i - 1)
                    act.activation(probs_T[:, i % 2, :], bank[2 + i % 2][:, 0:KEYS], ACT.Copy).then_inc(probsT_ready, 1)

                def take_o(p):
                    act.wait_ge(pv_done, HEADS * l + 2 * p + 2)
                    act.activation(oT[:, p, :], bank[7][:, 0:S], ACT.Copy).then_inc(oT_ready, 1)

                for i in range(HEADS + 2):
                    if i < HEADS:
                        exps(i)
                    if 1 <= i <= HEADS:
                        take_probs(i - 1)
                    if i >= 2 and i % 2 == 1:
                        take_o((i - 2) // 2)

            for l in range(LAYERS):
                norm(3 * l)
                take("in", l, lambda b, t, w: qkv[:, t, 512 * b:512 * b + w], ACT.Copy)
                act.wait_ge(proj_taken, act_evacs(blocks_of("in", l)[-1]))
                for u in range(4):
                    r, t = QK_RUN[l][u // 2], u % 2
                    act.activation(squares[:, u, :, :].rearrange("p n d -> p (n d)"), qkv[:, t, r:r + HEADS * DH],
                                   ACT.Square).then_inc(qk_squared, 1)
                act.wait_ge(h_var_ready, l + 1)
                act.activation(h_rstd[:], h_inv_var[:], ACT.Sqrt).then_inc(h_rstd_ready, 1)
                for p in range(PAIRS):
                    act.wait_ge(qk_turned, PAIRS * l + p + 1)
                    act.activation(qkT[:, p, :, :].rearrange("p k t -> p (k t)"), bank[4 + p % 2][:, :],
                                   ACT.Copy).then_inc(qkT_ready, 1)
                if l == 0:
                    for t in range(NT):
                        act.wait_ge(idx_turned, t + 1)
                        act.activation(idxT[:, :, P * t:P * t + P], bank[6 + t][:, 0:3 * P].rearrange("p (a t) -> p a t", a=3),
                                       ACT.Copy).then_inc(idxT_ready, 1)
                heads(l)
                norm(3 * l + 1)
                take("query", l, lambda b, t, w: qryT[:, 4 * b + 2 * t:4 * b + 2 * t + 2, :].rearrange("p a t -> p (a t)"), ACT.Copy)
                for g in range(4):
                    act.wait_ge(keys_scored, 8 * l + g + 1)
                    act.activation(key_s[:, 4 * g:4 * g + 4, :].rearrange("p a k -> p (a k)"), bank[4 + g][:, :],
                                   ACT.Copy).then_inc(key_s_ready, 1)
                with act.Fori(0, NK // 2) as k:
                    for s in range(2):
                        act.wait_ge(u_done, NK * l + k * 2 + s + 1)
                        act.activation(act_ijt[:, bass.ds(k * 2 + s, 1), :].rearrange("p a t -> p (a t)"), bank[4 + s][:, 0:S],
                                       ACT.Gelu_apprx_tanh).then_inc(gelu_done, 1)
                for t in range(NT):
                    act.wait_ge(cand_ready, 2 * l + t + 1)
                    act.activation(e_g[:, t, :, :], cv[:, t, :, :], ACT.Exp).then_inc(gexp_done, 1)
                act.wait_ge(gated_done, 64 * (l + 1) + 2)
                with act.Fori(0, NK // 2) as k:
                    for s in range(2):
                        act.wait_ge(v_done, NK * l + k * 2 + s + 1)
                        act.activation(wbuf[:, s, :], act_ijt[:, bass.ds(k * 2 + s, 1), :].rearrange("p a t -> p (a t)"),
                                       ACT.Copy).then_inc(w_ready, 1)
                norm(3 * l + 2)
                take("gate", l, lambda b, t, w: sig[:, t, 512 * b:512 * b + 512], ACT.Sigmoid)

        @block.vector
        def _(dve):
            steps = [0]

            def link(ins):
                steps[0] += 1
                ins.then_inc(dve_step, 1)
                dve.wait_ge(dve_step, steps[0])

            dve.sem_inc(gated_done, 2)
            dve.wait_ge(const_loaded, 16 * CONSTS)
            link(dve.tensor_copy(pos_f[:], pos_i[:]))
            for t in range(NT):
                ins = dve.tensor_scalar(rope_a[:, 2, t, :], inv_freq[:], pos_f[:, t:t + 1], None, ALU.mult)
            link(ins)
            for i in range(2):
                src = rope_a[:, 2, :, :]
                link(dve.tensor_scalar(rope_a[:, 3, :, :], src, 1.0 / (2 * np.pi), 0.25 * i, ALU.mult, ALU.add))
                link(dve.tensor_scalar(rope_a[:, 3, :, :], rope_a[:, 3, :, :], ROUND, -ROUND, ALU.add, ALU.add))
                for part in TWO_PI_PARTS:
                    link(dve.scalar_tensor_tensor(rope_a[:, i, :, :], rope_a[:, 3, :, :], -part, src, ALU.mult, ALU.add))
                    src = rope_a[:, i, :, :]
                if i:
                    link(dve.tensor_scalar(src, src, np.pi / 2, None, ALU.add))
                link(dve.tensor_scalar(src, src, 3.1415925, -3.1415925, ALU.min, ALU.max))
            dve.sem_inc(angle_ready, 1)
            dve.wait_ge(rope_ready, 1)
            dve.tensor_scalar(rope_sin[:, :, 0:HALF], rope_sin[:, :, HALF:ROT], -1.0, None, ALU.mult)
            link(dve.tensor_copy(rope_cos[:, :, HALF:ROT], rope_cos[:, :, 0:HALF]))

            def norm(n):
                if n:
                    dve.wait_ge(h_written, 4 * n)
                else:
                    dve.wait_ge(h_loaded, 16 * NT)
                dve.wait_ge(sumsq_done, 2 * (n + 1))
                link(dve.tensor_scalar(sumsq[:], sumsq[:], 1.0 / D, EPS, ALU.mult, ALU.add))
                dve.reciprocal(inv_var[:], sumsq[:]).then_inc(var_ready, 1)
                dve.wait_ge(rstd_ready, n + 1)
                for t in range(NT):
                    dve.tensor_scalar(xs[:, t, :], h[:, t, :], rstd[:, t:t + 1], None, ALU.mult).then_inc(xs_ready, 1)
                for c in range(4):
                    dve.wait_ge(xs_turned, 4 * n + c // 2 + 1)
                    dve.tensor_scalar(xnT[:, c, :], bank[4 + c // 2][:, S * (c % 2):S * (c % 2) + S], gain[:, n * NC + c:n * NC + c + 1], None,
                                      ALU.mult).then_inc(xnT_by_dve, 1)

            def rope(x, n, t):
                def table(v):
                    return v.unsqueeze(1).broadcast_to([P, n, v.shape[-1]])
                dve.tensor_tensor(rope_t[:, 0, 0:n, :], x[:, :, 0:ROT], table(rope_cos[:, t, :]), ALU.mult)
                dve.tensor_tensor(rope_t[:, 1, 0:n, 0:HALF], x[:, :, HALF:ROT], table(rope_sin[:, t, 0:HALF]), ALU.mult)
                link(dve.tensor_tensor(rope_t[:, 1, 0:n, HALF:ROT], x[:, :, 0:HALF], table(rope_sin[:, t, HALF:ROT]), ALU.mult))
                return dve.tensor_tensor(x[:, :, 0:ROT], rope_t[:, 0, 0:n, :], rope_t[:, 1, 0:n, :], ALU.add)

            def prepare_qk(l):
                for u in range(4):
                    dve.wait_ge(qk_squared, 4 * l + u + 1)
                    ins = dve.tensor_reduce(h_sumsq[:, u, :], squares[:, u, :, :], AX_X, ALU.add)
                link(ins)
                link(dve.tensor_scalar(h_sumsq[:], h_sumsq[:], 1.0 / DH, EPS, ALU.mult, ALU.add))
                dve.reciprocal(h_inv_var[:], h_sumsq[:]).then_inc(h_var_ready, 1)
                if l == 0:
                    dve.wait_ge(proj_taken, act_evacs(blocks_of("in", l)[-1]))
                    for t in range(NT):
                        x = qkv[:, t, IDX_COL:WI_COL].rearrange("p (n d) -> p n d", d=DH)
                        link(rope(x, IDX_HEADS + 1, t))
                        dve.tensor_copy(kk[:, t, :].rearrange("p (b d) -> p b d", b=2),
                                        x[:, IDX_HEADS:IDX_HEADS + 1, :].broadcast_to([P, 2, DH])).then_inc(idx_ready, 1)
                dve.wait_ge(h_rstd_ready, l + 1)
                for u in range(4):
                    r, t = QK_RUN[l][u // 2], u % 2
                    x = qkv[:, t, r:r + HEADS * DH].rearrange("p (n d) -> p n d", d=DH)
                    link(dve.tensor_tensor(x, x, h_rstd[:, u, :].unsqueeze(2).broadcast_to([P, HEADS, DH]), ALU.mult))
                    x4 = x.rearrange("p (b n) d -> p b n d", b=2)
                    link(dve.tensor_tensor(x4, x4, head_gain[:, l, u // 2, :, :].unsqueeze(2).broadcast_to([P, 2, 8, DH]),
                                           ALU.mult))
                    rope(x, HEADS, t).then_inc(qk_ready, 1)

            def select_dsa():
                for t, (x, y) in enumerate(SEG):
                    dve.wait_ge(logits_done, t + 1)
                    for i in range(IDX_HEADS):
                        src = bank[6][:, P * i:P * i + P] if t == 0 else bank[4 + i // 2][:, S * (i % 2):S * (i % 2) + S]
                        dst = idx_r if i else idx_s
                        link(dve.tensor_scalar(dst[:, x:y], src, 0.0, qkv[:, t, WI_COL + i:WI_COL + i + 1], ALU.max, ALU.mult))
                        if i:
                            link(dve.tensor_tensor(idx_s[:, x:y], idx_s[:, x:y], idx_r[:, x:y], ALU.add))
                    link(dve.tensor_tensor(idx_s[:, x:y], idx_s[:, x:y], bias_causal[:, x:y], ALU.add))
                    for _ in range(DSA_TOPK // 8):
                        link(dve.max(out=top8[:], in_=idx_s[:, x:y]))
                        link(dve.match_replace(out=idx_s[:, x:y], in_to_replace=top8[:], in_values=idx_s[:, x:y], imm_value=GONE))
                    link(dve.tensor_scalar(idx_r[:, x:y], idx_s[:, x:y], GONE / 2, NEG, ALU.is_gt, ALU.mult))
                    link(dve.tensor_tensor(bias_dsa[:, x:y], idx_r[:, x:y], bias_causal[:, x:y], ALU.add))

            def heads(l):
                def bias(i):
                    mask = bias_dilated if l else (bias_causal if i < 8 else bias_dsa)
                    dve.wait_ge(scores_done, HEADS * l + i + 1)
                    if i >= 2:
                        dve.wait_ge(exp_done, 2 * (HEADS * l + i - 1))
                    dve.scalar_tensor_tensor(biased[:, i % 2, :], bank[i % 2][:, 0:KEYS], SCALE, mask[:], ALU.mult,
                                             ALU.add).then_inc(biased_ready, 1)
                    dve.wait_ge(biased_ready, HEADS * l + i + 1)
                    for t, (x, y) in enumerate(SEG):
                        dve.tensor_reduce(neg_max[:, i % 2, t:t + 1], biased[:, i % 2, x:y], AX_X, ALU.max,
                                          negate=True).then_inc(negmax_ready, 1)

                def scale(i):
                    dve.wait_ge(exp_done, 2 * (HEADS * l + i + 1))
                    if i >= 2:
                        dve.wait_ge(probs_turned, HEADS * l + i - 1)
                    link(dve.reciprocal(inv_denom[:, i % 2, :], denom[:, i % 2, :]))
                    for t, (x, y) in enumerate(SEG):
                        dve.tensor_scalar(probs_n[:, i % 2, x:y], probs[:, i % 2, x:y], inv_denom[:, i % 2, t:t + 1], None,
                                          ALU.mult).then_inc(probs_ready, 1)

                for i in range(HEADS + 1):
                    if l == 0 and i == 8:
                        select_dsa()
                    if i < HEADS:
                        bias(i)
                    if i >= 1:
                        scale(i - 1)

            def add_blocks(kind, l):
                for n in blocks_of(kind, l):
                    b = BLOCKS[n][2]
                    for t in range(NT):
                        dve.wait_ge(proj_done, 2 * n + t + 1)
                        x = h[:, t, 512 * b:512 * b + 512]
                        y = bank[2 * (n % 2) + t][:, :]
                        if kind == "up":
                            gate = sig[:, t, 512 * b:512 * b + 512]
                            link(dve.tensor_tensor(gate, y, gate, ALU.mult))
                            y = gate
                        dve.tensor_tensor(x, x, y, ALU.add).then_inc(h_written, 1)

            def top16(values, indices, src):
                link(dve.max(out=values[:, 0:8], in_=src))
                dve.max_index(out=indices[:, 0:8], in_max=values[:, 0:8], in_values=src)
                link(dve.match_replace(out=src, in_to_replace=values[:, 0:8], in_values=src, imm_value=GONE))
                link(dve.max(out=values[:, 8:16], in_=src))
                return dve.max_index(out=indices[:, 8:16], in_max=values[:, 8:16], in_values=src)

            def select_experts(l):
                for t in range(NT):
                    for a_ in range(HC):
                        if t == 0:
                            dve.wait_ge(key_s_ready, 4 * l + a_ // 4 + 1)
                            src = key_s[:, a_, :]
                        else:
                            dve.wait_ge(keys_scored, 8 * l + 4 + a_ // 4 + 1)
                            src = bank[a_ // 4][:, NK * (a_ % 4):NK * (a_ % 4) + NK]
                        ins = top16(sv[:, a_, :], si[:, a_, :], src)
                    link(ins)
                    halves = sv[:, :, :].rearrange("p (g c) k -> p g c k", c=2)
                    link(dve.tensor_tensor(cand, halves[:, :, 0, :].unsqueeze(3).broadcast_to([P, PH, TOPK, TOPK]),
                                           halves[:, :, 1, :].unsqueeze(2).broadcast_to([P, PH, TOPK, TOPK]), ALU.add))
                    dve.tensor_copy(si_f[:], si[:])
                    for g in range(PH):
                        ins = top16(cv[:, t, g, :], ci[:, g, :], cand[:, g, :, :].rearrange("p a b -> p (a b)"))
                    link(ins)
                    dve.tensor_scalar(rank[:, 0, :, :], ci[:], 4, None, ALU.logical_shift_right)
                    link(dve.tensor_scalar(rank[:, 1, :, :], ci[:], 15, None, ALU.bitwise_and))
                    link(dve.tensor_copy(rank_f[:], rank[:]))
                    idx = si_f[:, :, :].rearrange("p (g c) k -> p g c k", c=2)
                    for c, e in enumerate((e_i, e_j)):
                        link(dve.tensor_tensor(eq, rank_f[:, c, :, :].unsqueeze(3).broadcast_to([P, PH, TOPK, TOPK]),
                                               iota[:, 0:TOPK].unsqueeze(1).unsqueeze(1).broadcast_to([P, PH, TOPK, TOPK]),
                                               ALU.is_equal))
                        link(dve.tensor_tensor(eq, eq, idx[:, :, c, :].unsqueeze(2).broadcast_to([P, PH, TOPK, TOPK]), ALU.mult))
                        link(dve.tensor_reduce(e[:, t, :, :], eq, AX_X, ALU.add))
                    link(dve.tensor_reduce(g_inv[:, t, :], cv[:, t, :, :], AX_X, ALU.max))
                    dve.tensor_tensor(cv[:, t, :, :], cv[:, t, :, :], g_inv[:, t, :].unsqueeze(2).broadcast_to([P, PH, TOPK]),
                                      ALU.subtract).then_inc(cand_ready, 1)
                for t in range(NT):
                    dve.wait_ge(gexp_done, 2 * l + t + 1)
                    link(dve.tensor_reduce(g_sum[:, t, :], e_g[:, t, :, :], AX_X, ALU.add))
                    link(dve.reciprocal(g_inv[:, t, :], g_sum[:, t, :]))
                    dve.tensor_tensor(e_g[:, t, :, :], e_g[:, t, :, :], g_inv[:, t, :].unsqueeze(2).broadcast_to([P, PH, TOPK]),
                                      ALU.mult).then_inc(sel_ready, 1)
                for t in range(NT):
                    dve.wait_ge(sel_turned, 2 * l + t + 1)
                    dve.tensor_copy(ijgT[:, :, P * t:P * t + P], bank[6 + t][:, 0:3 * P].rearrange("p (e t) -> p e t", e=3)) \
                       .then_inc(selT_ready, 1)
                dve.wait_ge(selT_ready, 2 * (l + 1))

            def gate_groups(l):
                def hot(k, s):
                    dve.wait_ge(gates_done, 64 * l + k * 2 + s + 1)
                    for q in range(4):
                        t = k * 8 + (4 * s + q)
                        ins = dve.tensor_scalar(hot_i[:, s, q, :], iota[:], ijgT[:, 0, bass.ds(t, 1)],
                                                ijgT[:, 2, bass.ds(t, 1)], ALU.is_equal, ALU.mult)
                    ins.then_inc(hot_i_ready, 1)
                    for q in range(4):
                        t = k * 8 + (4 * s + q)
                        ins = dve.tensor_scalar(hot_j[:, s, q, :], iota[:], ijgT[:, 1, bass.ds(t, 1)], None, ALU.is_equal)
                    ins.then_inc(hot_j_ready, 1)

                def multiply(k, s):
                    dve.wait_ge(gates_done, 64 * l + k * 2 + s + 3)
                    x = act_itj[:, bass.ds(k * 8 + 4 * s, 4), :]
                    dve.tensor_tensor(x, x, bank[4 + s][:, :].rearrange("p (q j) -> p q j", q=4),
                                      ALU.mult).then_inc(gated_done, 1)

                with dve.Fori(0, S // 8) as k:
                    hot(k, 0)
                    hot(k, 1)
                    multiply(k, 0)
                    multiply(k, 1)

            for l in range(LAYERS):
                norm(3 * l)
                prepare_qk(l)
                heads(l)
                add_blocks("out", l)
                norm(3 * l + 1)
                select_experts(l)
                gate_groups(l)
                dve.wait_ge(v_done, NK * (l + 1) + 2)
                for t in range(NT):
                    for b in range(2):
                        x = h[:, t, 512 * b:512 * b + 512]
                        dve.tensor_tensor(x, x, bank[2 * t + b][:, :], ALU.add).then_inc(h_written, 1)
                norm(3 * l + 2)
                dve.wait_ge(proj_taken, act_evacs(blocks_of("gate", l)[-1]))
                add_blocks("up", l)


def blocked(w):
    k, n = w.shape
    w = w.reshape(k // P, P, n).transpose(1, 0, 2)
    return np.concatenate([w[:, :, b:b + 512].reshape(P, -1) for b in range(0, n, 512)], axis=1)


def shape_constants():
    t = np.arange(P)[:, None]
    causal, dilated = [], []
    for tile, (x, y) in enumerate(SEG):
        dist = t + P * tile - np.arange(y - x)[None, :]
        count = np.zeros(dist.shape, np.int64)
        for window, dil in ((128, 1), (512, 4), (2048, 16)):
            count += (dist >= 0) & (dist <= window) & (dist % dil == 0)
        causal.append(np.where(dist >= 0, 0.0, NEG))
        dilated.append(np.where(count > 0, np.log(np.maximum(count, 1)), NEG))
    half = np.arange(HALF, dtype=np.float32)
    inv = np.power(np.float32(500000.0), -half / np.float32(HALF)).astype(np.float32)
    return {
        "ident": np.eye(P, dtype=np.float32),
        "iota": np.tile(np.arange(P, dtype=np.float32), (P, 1)),
        "bias_causal": np.concatenate(causal, axis=1).astype(np.float32),
        "bias_dilated": np.concatenate(dilated, axis=1).astype(np.float32),
        "inv_freq": np.tile(inv, (P, 1)),
    }


def lay_out(i):
    a = shape_constants()
    c = np.ascontiguousarray
    a["x"] = c(i["x"][0])
    a["positions"] = c(i["positions"][0].reshape(NT, P).T)
    gains = np.stack([i[n][l] for l in range(LAYERS) for n in ("attn_norm", "ffn_norm", "ple_norm")])
    a["gain"] = c(gains.reshape(3 * LAYERS * NC, P).T)
    hg = np.stack([i["a_q_norm"][0], i["a_k_norm"][0], i["b_q_norm"][0], i["b_k_norm"][0],
                   i["c_q_norm"][0], i["c_q_norm"][0], i["c_k_norm"][0], i["c_k_norm"][0]])
    a["head_gain"] = c(np.broadcast_to(hg.reshape(1, LAYERS, 2, 2, DH), (P, LAYERS, 2, 2, DH)))
    for l, (w_in, w_out) in enumerate((("ab_w_in", "ab_w_out"), ("c_w_in", "c_w_out"))):
        a[f"in{l}"] = blocked(i[w_in][0])
        a[f"out{l}"] = blocked(i[w_out][0])
        a[f"query{l}"] = blocked(i["peer_w_query"][l])
        a[f"gate{l}"] = blocked(i["ple_w_gate"][l])
        up = i["ple_w_up"][l].reshape(2, P, 2, 512).transpose(1, 2, 0, 3).reshape(P, 2, -1)
        emb = i["p"][l, 0].T.reshape(2, P, S).transpose(1, 0, 2).reshape(P, -1)
        a[f"up{l}"] = np.concatenate([up[:, 0], emb, up[:, 1], emb], axis=1)
    a["keysT"] = c(i["peer_sub_keys"].reshape(LAYERS, HC, NK, P).transpose(0, 3, 1, 2))
    a["uT"] = c(i["peer_u"].reshape(LAYERS, NK, NK, NC, P).transpose(0, 2, 4, 3, 1)).reshape(LAYERS, NK, P, D)
    a["v"] = c(i["peer_v"].reshape(LAYERS, NK, NK, D).transpose(0, 2, 1, 3))
    return a


def kernel(**inputs):
    import concourse.bacc as bacc
    from concourse.bass_utils import run_bass_kernel_spmd

    arrays = lay_out({k: np.asarray(v) for k, v in inputs.items()})
    nc = bacc.Bacc("TRN2", target_bir_lowering=False, num_devices=1)
    aps = {k: nc.dram_tensor(f"in_{k}", v.shape, mybir.dt.from_np(v.dtype), kind="ExternalInput").ap()
           for k, v in arrays.items()}
    out = nc.dram_tensor("out", (S, D), F32, kind="ExternalOutput").ap()
    hybrid_trunk(nc, aps, out)
    r = run_bass_kernel_spmd(nc, [{f"in_{k}": v for k, v in arrays.items()}], core_ids=[0])
    return r.results[0]["out"].reshape(1, S, D)
```

```python
from contextlib import ExitStack

import numpy as np

import concourse.bass as bass
from concourse import mybir

ALU = mybir.AluOpType
ACT = mybir.ActivationFunctionType
F32 = mybir.dt.float32
F32R = mybir.dt.float32r
BF16 = mybir.dt.bfloat16
U32 = mybir.dt.uint32
I32 = mybir.dt.int32
AX_X = mybir.AxisListType.X

P = 128
D = 1024
S = 256
NT = S // P
NC = D // P
LAYERS = 2
DH = 64
ROT = 16
HALF = ROT // 2
EPS = 1e-6
NEG = -1e30
GONE = -3e38
HEADS = 16
PAIRS = HEADS // 2
IN_WIDTH = (3396, 3072)
V_COL = ([1024 + DH * h for h in range(8)] + [2560 + DH * h for h in range(8)],
         [2048 + DH * h for h in range(16)])
QK_RUN = ((0, 1536), (0, 1024))
Q_COL = ([128 * p for p in range(4)] + [1536 + 128 * p for p in range(4)], [128 * p for p in range(8)])
K_COL = ([512 + 128 * p for p in range(4)] + [2048 + 128 * p for p in range(4)],
         [1024 + 128 * p for p in range(8)])
IDX_COL, IDX_HEADS, WI_COL = 3072, 4, 3392
DSA_TOPK = 64
PH = 8
HC = 2 * PH
NK = 128
TOPK = 16
KEYS = P + 2 * P
SEG = ((0, P), (P, 3 * P))
SCALE = DH ** -0.5
TWO_PI_PARTS = (6.28125, 1.9350051879882812e-03, 3.0199159819567529e-07)
ROUND = 12582912.0

PIECE = 1024
SLOTS = 4
LO_SLOTS = 2
AHEAD = 3
J_HALF = NK // 2
IN_ORDER = ([6, 0, 1, 3, 4, 2, 5], [0, 1, 2, 3, 4, 5])


def stream_plan():
    plan, at = [], 0
    for l in range(LAYERS):
        part = {}
        for kind, n in (("in", 4 * len(IN_ORDER[l])), ("out", 8), ("query", HC), ("u", NK), ("v", NK),
                        ("gate", 8), ("up", 4)):
            part[kind] = at
            at += n
        plan.append(part)
    return plan, at


PLAN, PIECES = stream_plan()
assert PIECES % SLOTS == 0 and all(v % SLOTS == 0 for part in PLAN for v in part.values())
TAKEN = [0, 2 * (len(IN_ORDER[0]) + 2)]


def hybrid_trunk(nc, a, out):
    with ExitStack() as ctx:
        def sb(name, shape, dt=F32):
            return ctx.enter_context(nc.sbuf_tensor(name, shape, dt))

        def sem(name):
            return ctx.enter_context(nc.semaphore(name))

        h = sb("h", [P, NT, D])
        x_hi = sb("x_hi", [P, NC, S], F32R)
        x_lo = sb("x_lo", [P, NC, S], F32R)
        raw = sb("raw", [P, SLOTS, PIECE])
        w_hi = sb("w_hi", [P, SLOTS, PIECE], F32R)
        w_lo = sb("w_lo", [P, LO_SLOTS, PIECE], F32R)
        arena = sb("arena", [P, P * S])
        hot_i = sb("hot_i", [P, 2, 4, P], BF16)
        hot_j = sb("hot_j", [P, 2, 4, J_HALF], BF16)
        hot_jg = sb("hot_jg", [P, 2, 3, 4, J_HALF], BF16)
        ident = sb("ident", [P, P])
        iota = sb("iota", [P, P])
        iota_bf = sb("iota_bf", [P, P], BF16)
        gain = sb("gain", [P, 3 * LAYERS * NC])
        inv_freq = sb("inv_freq", [P, HALF])
        pos_i = sb("pos_i", [P, NT], I32)
        pos_f = sb("pos_f", [P, NT])
        rope_a = sb("rope_a", [P, 4, NT, HALF])
        rope_cos = sb("rope_cos", [P, NT, ROT])
        rope_sin = sb("rope_sin", [P, NT, ROT])
        sumsq = sb("sumsq", [P, NT])
        inv_var = sb("inv_var", [P, NT])
        rstd = sb("rstd", [P, NT])
        h_sumsq = sb("h_sumsq", [P, 2 * NT, HEADS])
        h_inv_var = sb("h_inv_var", [P, 2 * NT, HEADS])
        h_rstd = sb("h_rstd", [P, 2 * NT, HEADS])
        top8 = sb("top8", [P, 8])
        neg_max = sb("neg_max", [P, 2, NT])
        denom = sb("denom", [P, 2, NT])
        inv_denom = sb("inv_denom", [P, 2, NT])
        cv = sb("cv", [P, NT, PH, TOPK])
        e_g = sb("e_g", [P, NT, PH, TOPK])
        g_sum = sb("g_sum", [P, NT, PH])
        g_inv = sb("g_inv", [P, NT, PH])
        ijT = sb("ijT", [P, 2, S], BF16)
        gT = sb("gT", [P, 3, S], BF16)
        g_rest = sb("g_rest", [P, 2, S])

        x_hi_f, w_hi_f = (v.bitcast(F32) for v in (x_hi[:, :, :], w_hi[:, :, :]))
        g_hi, g_lo, g_hi_f = (v[:, 0:2, :] for v in (x_hi, x_lo, x_hi_f))

        at = [0]

        def region(*shape, dt=F32):
            n = int(np.prod(shape))
            at[0] += n
            assert at[0] <= P * S
            v = arena[:, at[0] - n:at[0]]
            v = v if dt is F32 else v.bitcast(dt)
            names = "abcd"[:len(shape)]
            return v.rearrange(f"p ({' '.join(names)}) -> p {' '.join(names)}", **dict(zip(names, shape)))

        xs = region(NT, D)
        qkv = region(NT, IN_WIDTH[0])
        sig = region(NT, D)
        kk = region(NT, P)
        idxT = region(3, S)
        idx_s = region(KEYS)
        idx_r = region(KEYS)
        bias_dsa = region(KEYS)
        rope_t = region(2, HEADS, ROT)
        mask_bias = region(KEYS)
        head_gain = region(2, 2, DH)
        at[0] = max(at[0], J_HALF * S)
        upper = at[0]
        qkT = region(PAIRS, 2, S)
        squares = region(2 * NT, HEADS, DH)
        biased = region(2, KEYS)
        probs = region(2, KEYS)
        probs_n = region(2, KEYS)
        probs_T = region(2, KEYS)
        at[0] = upper
        qryT = region(HC, S)
        key_s = region(HC, NK)
        cand = region(PH, TOPK, TOPK)
        eq = region(PH, TOPK, TOPK)
        sv = region(HC, TOPK)
        si = region(HC, TOPK, dt=U32)
        si_f = region(HC, TOPK)
        ci = region(PH, TOPK, dt=U32)
        rank = region(2, PH, TOPK, dt=U32)
        rank_f = region(2, PH, TOPK)
        e_i = region(NT, PH, TOPK)
        e_j = region(NT, PH, TOPK)
        keysT = region(HC, NK)
        act_ijt = arena[:, :].rearrange("p (j t) -> p j t", t=S)
        act_itj = arena[:, :].rearrange("p (j t) -> p t j", t=S)

        bank = [ctx.enter_context(nc.psum_tensor(f"bank{i}", [P, 512], F32)) for i in range(8)]

        const_loaded = sem("const_loaded")
        h_loaded = sem("h_loaded")
        angle_ready = sem("angle_ready")
        rope_ready = sem("rope_ready")
        piece_loaded = [sem(f"piece_loaded{i}") for i in range(SLOTS)]
        hi_ready = sem("hi_ready")
        lo_ready = sem("lo_ready")
        piece_used = sem("piece_used")
        layer_loaded = sem("layer_loaded")
        stored = sem("stored")
        sumsq_done = sem("sumsq_done")
        var_ready = sem("var_ready")
        rstd_ready = sem("rstd_ready")
        xs_ready = sem("xs_ready")
        xs_turned = sem("xs_turned")
        x_hi_ready = sem("x_hi_ready")
        x_lo_ready = sem("x_lo_ready")
        proj_taken = sem("proj_taken")
        h_written = sem("h_written")
        qk_squared = sem("qk_squared")
        h_var_ready = sem("h_var_ready")
        h_rstd_ready = sem("h_rstd_ready")
        qk_ready = sem("qk_ready")
        idx_ready = sem("idx_ready")
        qk_turned = sem("qk_turned")
        qkT_ready = sem("qkT_ready")
        idx_turned = sem("idx_turned")
        idxT_ready = sem("idxT_ready")
        even_logits = sem("even_logits")
        logits_done = sem("logits_done")
        logits_taken = sem("logits_taken")
        scores_done = sem("scores_done")
        biased_ready = sem("biased_ready")
        negmax_ready = sem("negmax_ready")
        exp_done = sem("exp_done")
        probs_ready = sem("probs_ready")
        probs_turned = sem("probs_turned")
        probsT_ready = sem("probsT_ready")
        pv_done = sem("pv_done")
        o_hi_ready = sem("o_hi_ready")
        o_lo_ready = sem("o_lo_ready")
        qryT_ready = sem("qryT_ready")
        keys_scored = sem("keys_scored")
        key_s_ready = sem("key_s_ready")
        gelu_done = sem("gelu_done")
        cand_ready = sem("cand_ready")
        gexp_done = sem("gexp_done")
        sel_ready = sem("sel_ready")
        sel_turned = sem("sel_turned")
        hot_j_ready = sem("hot_j_ready")
        hot_ready = sem("hot_ready")
        gates_done = sem("gates_done")
        gated_done = sem("gated_done")
        g_hi_ready = sem("g_hi_ready")
        g_lo_ready = sem("g_lo_ready")
        dve_step = sem("dve_step")

        block = ctx.enter_context(nc.Block())
        CONSTS = 5


        @block.sync
        def _(sp):
            for i in range(NT):
                sp.dma_start(h[:, i, :], a["x"][P * i:P * i + P, :]).then_inc(h_loaded, 16)
            for dst, src in ((inv_freq[:], a["inv_freq"]), (pos_i[:], a["positions"]), (ident[:], a["ident"]),
                             (gain[:], a["gain"]), (iota[:], a["iota"])):
                sp.dma_start(dst, src).then_inc(const_loaded, 16)
            with sp.Fori(0, PIECES // SLOTS) as k:
                for c in range(SLOTS):
                    sp.wait_ge(hi_ready, k * SLOTS + c + 1)
                    sp.wait_ge(lo_ready, k * SLOTS + c + 1)
                    sp.dma_start(raw[:, c, :], a["stream"][bass.ds(k * SLOTS + c, 1), :, :]
                                 .rearrange("a p n -> (a p) n")).then_inc(piece_loaded[c], 16)
            sp.wait_ge(h_written, 12 * LAYERS)
            for i in range(NT):
                sp.dma_start(out[P * i:P * i + P, :], h[:, i, :]).then_inc(stored, 16)
            sp.wait_ge(stored, 16 * NT)

        @block.gpsimd
        def _(pool):
            pool.sem_inc(lo_ready, SLOTS)
            with pool.Fori(0, PIECES // SLOTS) as k:
                for c in range(SLOTS):
                    pool.wait_ge(hi_ready, k * SLOTS + c + 1 + SLOTS)
                    pool.wait_ge(piece_used, k * SLOTS + c + 1 + SLOTS - LO_SLOTS)
                    pool.tensor_tensor(w_lo[:, c % LO_SLOTS, :], raw[:, c, :], w_hi_f[:, c, :], ALU.subtract) \
                        .then_inc(lo_ready, 1)

        @block.tensor
        def _(pe):
            pe.sem_inc(piece_used, SLOTS)
            pe.sem_inc(gates_done, 2)
            pe.wait_ge(const_loaded, 16 * CONSTS)

            def multiply(c, k, terms, w_moves=True):
                hi, lo = w_hi[:, c % SLOTS, :], w_lo[:, c % LO_SLOTS, :]
                pe.wait_ge(hi_ready, k * SLOTS + c + 1 + SLOTS)
                for dst, x, cols, first, _ in terms:
                    for i in range(2):
                        st, mv = (x[i], hi[:, cols]) if w_moves else (hi[:, cols], x[i])
                        pe.matmul(dst, st, mv, start=first and i == 0, stop=False)
                pe.wait_ge(lo_ready, k * SLOTS + c + 1 + SLOTS)
                for dst, x, cols, _, last in terms:
                    st, mv = (x[0], lo[:, cols]) if w_moves else (lo[:, cols], x[0])
                    mm = pe.matmul(dst, st, mv, start=False, stop=last)
                mm.then_inc(piece_used, 1)

            def turn_normed(n):
                pe.wait_ge(xs_ready, 2 * (n + 1))
                for g in range(4):
                    for c in (2 * g, 2 * g + 1):
                        for t in range(NT):
                            q = (c % 2) * S + t * P
                            mm = pe.transpose(bank[4 + g][:, q:q + P], xs[:, t, c * P:c * P + P], ident[:])
                    mm.then_inc(xs_turned, 1)

            def await_x(n):
                pe.wait_ge(x_hi_ready, NC * (n + 1))
                pe.wait_ge(x_lo_ready, NC * (n + 1))

            def project(m, i, width=512):
                for q in range(4):
                    multiply(m + q, 0, [(bank[2 * (i % 2) + t][:, 0:width],
                                         [v[:, 2 * q + c, P * t:P * t + P] for v in (x_hi, x_lo)],
                                         slice(512 * c, 512 * c + width), q == 0 and c == 0, q == 3 and c == 1)
                                        for t in range(NT) for c in range(2)])

            def turned_project(c, k, dst):
                multiply(c, k, [(dst, [v[:, i, :] for v in (x_hi, x_lo)], slice(P * i, P * i + P), i == 0, i == NC - 1)
                                for i in range(NC)], w_moves=False)

            def index_logits():
                pe.wait_ge(idx_ready, NT)
                for t in range(NT):
                    for i in range(3):
                        src = kk[:, t, :] if i == 2 else qkv[:, t, IDX_COL + P * i:IDX_COL + P * i + P]
                        mm = pe.transpose(bank[6 + t][:, P * i:P * i + P], src, ident[:])
                    mm.then_inc(idx_turned, 1)
                pe.wait_ge(idxT_ready, NT)
                for t in range(NT):
                    for i in (0, 2, 1, 3):
                        o = DH * (i % 2)
                        if i == 1:
                            mm.then_inc(even_logits, 1)
                            pe.wait_ge(even_logits, t + 1)
                        dst = bank[6][:, P * i:P * i + P] if t == 0 else bank[4 + i // 2][:, S * (i % 2):S * (i % 2) + S]
                        mm = pe.matmul(dst, idxT[o:o + DH, i // 2, P * t:P * t + P],
                                       idxT[o:o + DH, 2, 0:P * (t + 1)], start=True, stop=True)
                    mm.then_inc(logits_done, 1)

            def project_in(l):
                for i, b in enumerate(IN_ORDER[l]):
                    if i >= 2:
                        pe.wait_ge(proj_taken, TAKEN[l] + 2 * (i - 1))
                    project(PLAN[l]["in"] + 4 * i, i, min(512, IN_WIDTH[l] - 512 * b))
                    if l == 0 and i == 1:
                        index_logits()

            def turn_qk(l):
                if l == 0:
                    pe.wait_ge(logits_taken, 1)
                for p in range(PAIRS):
                    pe.wait_ge(qk_ready, 4 * l + (2 * (1 + p // 4) if l == 0 else 4))
                    if p >= 2:
                        pe.wait_ge(qkT_ready, PAIRS * l + p - 1)
                    for i, col in enumerate((Q_COL[l][p], K_COL[l][p])):
                        for t in range(NT):
                            q = i * S + t * P
                            mm = pe.transpose(bank[4 + p % 2][:, q:q + P], qkv[:, t, col:col + P], ident[:])
                    mm.then_inc(qk_turned, 1)

            def heads(l):
                pe.wait_ge(qkT_ready, PAIRS * (l + 1))
                pe.wait_ge(proj_taken, TAKEN[l] + 2 * len(IN_ORDER[l]))

                def scores(i):
                    o, p = DH * (i % 2), i // 2
                    if i >= 2:
                        pe.wait_ge(biased_ready, HEADS * l + i - 1)
                    for t in range(NT):
                        mm = pe.matmul(bank[i % 2][:, SEG[t][0]:SEG[t][1]], qkT[o:o + DH, p, 0, P * t:P * t + P],
                                       qkT[o:o + DH, p, 1, 0:P * (t + 1)], start=True, stop=True)
                    mm.then_inc(scores_done, 1)

                def turn(i):
                    pe.wait_ge(probs_ready, 2 * (HEADS * l + i + 1))
                    if i >= 2:
                        pe.wait_ge(probsT_ready, HEADS * l + i - 1)
                    for q in range(3):
                        mm = pe.transpose(bank[2 + i % 2][:, P * q:P * q + P], probs_n[:, i % 2, P * q:P * q + P], ident[:])
                    mm.then_inc(probs_turned, 1)

                def pv(i):
                    o, p, c = DH * (i % 2), i // 2, V_COL[l][i]
                    pe.wait_ge(probsT_ready, HEADS * l + i + 1)
                    if i % 2 == 0 and p >= 2:
                        pe.wait_ge(o_lo_ready, PAIRS * l + p - 1)
                    for t in range(NT):
                        for s in range(t + 1):
                            q = SEG[t][0] + P * s
                            mm = pe.matmul(bank[6 + p % 2][o:o + DH, P * t:P * t + P],
                                           qkv[:, s, c:c + DH], probs_T[:, i % 2, q:q + P],
                                           start=(s == 0), stop=(s == t))
                    mm.then_inc(pv_done, 1)

                scores(0)
                for i in range(HEADS + 2):
                    if i + 1 < HEADS:
                        scores(i + 1)
                    if 1 <= i <= HEADS:
                        turn(i - 1)
                    if i >= 2:
                        pv(i - 2)

            def retrieve(l):
                for i in range(HC):
                    if i >= 4:
                        pe.wait_ge(qryT_ready, HC * l + i - 3)
                    turned_project(PLAN[l]["query"] + i, 0, bank[4 + i % 4][:, 0:S])
                pe.wait_ge(qryT_ready, HC * (l + 1))
                pe.wait_ge(layer_loaded, 48 * (l + 1))
                for u in range(2 * 4):
                    t, g = u // 4, u % 4
                    for i in range(4):
                        mm = pe.matmul(bank[4 * (1 - t) + g][:, P * i:P * i + P], qryT[:, 4 * g + i, P * t:P * t + P],
                                       keysT[:, 4 * g + i, :], start=True, stop=True)
                    mm.then_inc(keys_scored, 1)
                pe.wait_ge(key_s_ready, 4 * (l + 1))

            def chunk_u(l, j, k):
                pe.wait_ge(gelu_done, NK * l + k * SLOTS + j + 1)
                turned_project(PLAN[l]["u"] + j, k, bank[4 + j % 2][:, 0:S])

            def chunk_v(l, j, k, first=False, last=False):
                pe.wait_ge(g_hi_ready, NK * l + k * SLOTS + j + 1)
                pe.wait_ge(g_lo_ready, NK * l + k * SLOTS + j + 1)
                multiply(PLAN[l]["v"] + j, k, [(bank[2 * t + b][:, :], [v[:, j % 2, P * t:P * t + P] for v in (g_hi, g_lo)],
                                                slice(512 * b, 512 * b + 512), first, last)
                                               for t in range(NT) for b in range(2)])

            def gates(l, half, c, k):
                n = S // 4 * (2 * l + half) + c
                pe.wait_ge(hot_ready, n + k * SLOTS + 1)
                pe.wait_ge(gated_done, n + k * SLOTS + 1)
                for q in range(4):
                    for i in range(3):
                        mm = pe.matmul(bank[6 + c % 2][:, J_HALF * q:J_HALF * q + J_HALF], hot_i[:, c % 2, q, :],
                                       hot_jg[:, c % 2, i, q, :], start=i == 0, stop=i == 2)
                mm.then_inc(gates_done, 1)

            def turn_selected(l):
                for t in range(NT):
                    pe.wait_ge(sel_ready, 2 * l + t + 1)
                    for i, e in enumerate((e_i, e_j, e_g)):
                        mm = pe.transpose(bank[6 + t][:, P * i:P * i + P], e[:, t, :, :].rearrange("p g k -> p (g k)"), ident[:])
                    mm.then_inc(sel_turned, 1)

            def experts(l):
                quarter = J_HALF // SLOTS
                with pe.Fori(0, quarter) as k:
                    for c in range(SLOTS):
                        chunk_u(l, c, k)
                turn_selected(l)
                with pe.Fori(0, quarter) as k:
                    for c in range(SLOTS):
                        chunk_u(l, J_HALF + c, k)
                        gates(l, 0, c, k)
                for c in range(SLOTS):
                    chunk_v(l, c, 0, first=c == 0)
                    gates(l, 1, c, 0)
                with pe.Fori(1, quarter) as k:
                    for c in range(SLOTS):
                        chunk_v(l, c, k)
                        gates(l, 1, c, k)
                with pe.Fori(0, quarter - 1) as k:
                    for c in range(SLOTS):
                        chunk_v(l, J_HALF + c, k)
                for c in range(SLOTS):
                    chunk_v(l, NK - SLOTS + c, 0, last=c == SLOTS - 1)

            def embed(l):
                pe.wait_ge(proj_taken, TAKEN[l] + 2 * len(IN_ORDER[l]) + 4)
                for q in range(4):
                    m = PLAN[l]["up"] + q
                    pe.wait_ge(lo_ready, m + 1 + SLOTS)
                    multiply(m, 0, [(bank[2 * (q // 2) + t][:, S * (q % 2):S * (q % 2) + S],
                                     [v[:, 512 * c + P * t:512 * c + P * t + P]
                                      for v in (w_hi[:, m % SLOTS, :], w_lo[:, m % LO_SLOTS, :])],
                                     slice(512 * c + S, 512 * c + 2 * S), c == 0, c == 1)
                                    for t in range(NT) for c in range(2)])

            for l in range(LAYERS):
                turn_normed(3 * l)
                await_x(3 * l)
                project_in(l)
                turn_qk(l)
                heads(l)
                pe.wait_ge(o_lo_ready, PAIRS * (l + 1))
                for i in range(2):
                    project(PLAN[l]["out"] + 4 * i, i)
                turn_normed(3 * l + 1)
                await_x(3 * l + 1)
                retrieve(l)
                experts(l)
                turn_normed(3 * l + 2)
                await_x(3 * l + 2)
                for i in range(2):
                    project(PLAN[l]["gate"] + 4 * i, i)
                embed(l)

        @block.scalar
        def _(act):
            act.sem_inc(hi_ready, SLOTS)
            act.sem_inc(gelu_done, 2)
            split = [0]

            def split_hi(c, k=0):
                act.wait_ge(piece_loaded[c % SLOTS], (k + c // SLOTS + 1) * 16)
                act.wait_ge(piece_used, k * SLOTS + c + 1)
                act.activation(w_hi[:, c % SLOTS, :], raw[:, c % SLOTS, :], ACT.Copy).then_inc(hi_ready, 1)

            def split_to(m):
                while split[0] <= min(m, PIECES - 1):
                    split_hi(split[0])
                    split[0] += 1

            def multiplied(c, k=0):
                act.wait_ge(piece_used, k * SLOTS + c + 1 + SLOTS)

            act.wait_ge(const_loaded, 16 * CONSTS)

            def rope_tables():
                act.wait_ge(angle_ready, 1)
                act.activation(rope_sin[:, :, HALF:ROT], rope_a[:, 0, :, :], ACT.Sin)
                act.activation(rope_cos[:, :, 0:HALF], rope_a[:, 1, :, :], ACT.Sin).then_inc(rope_ready, 1)

            def norm(n):
                if n:
                    act.wait_ge(h_written, 4 * n)
                else:
                    act.wait_ge(h_loaded, 16 * NT)
                for t in range(NT):
                    act.activation(xs[:, t, :], h[:, t, :], ACT.Square, accum_out=sumsq[:, t:t + 1]).then_inc(sumsq_done, 1)
                act.wait_ge(var_ready, n + 1)
                act.activation(rstd[:], inv_var[:], ACT.Sqrt).then_inc(rstd_ready, 1)
                for c in range(NC):
                    act.wait_ge(xs_turned, 4 * n + c // 2 + 1)
                    act.activation(x_hi[:, c, :], bank[4 + c // 2][:, S * (c % 2):S * (c % 2) + S], ACT.Copy,
                                   scale=gain[:, n * NC + c:n * NC + c + 1]).then_inc(x_hi_ready, 1)

            def take_block(m, i, w, dst, func):
                split_to(m + 3 + AHEAD)
                multiplied(m + 3)
                for t in range(NT):
                    act.activation(dst(t), bank[2 * (i % 2) + t][:, 0:w], func).then_inc(proj_taken, 1)

            def square_run(l, r):
                for t in range(NT):
                    x = QK_RUN[l][r]
                    act.activation(squares[:, 2 * r + t, :, :].rearrange("p n d -> p (n d)"), qkv[:, t, x:x + HEADS * DH],
                                   ACT.Square).then_inc(qk_squared, 1)

            def root_run(l, r):
                act.wait_ge(h_var_ready, 2 * l + r + 1)
                act.activation(h_rstd[:, 2 * r:2 * r + 2, :], h_inv_var[:, 2 * r:2 * r + 2, :], ACT.Sqrt).then_inc(h_rstd_ready, 1)

            def heads(l):
                def exps(i):
                    act.wait_ge(negmax_ready, 2 * (HEADS * l + i + 1))
                    if i >= 2:
                        act.wait_ge(probs_ready, 2 * (HEADS * l + i - 1))
                    for t, (x, y) in enumerate(SEG):
                        act.activation(probs[:, i % 2, x:y], biased[:, i % 2, x:y], ACT.Exp,
                                       bias=neg_max[:, i % 2, t:t + 1],
                                       accum_out=denom[:, i % 2, t:t + 1]).then_inc(exp_done, 1)

                def take_probs(i):
                    act.wait_ge(probs_turned, HEADS * l + i + 1)
                    if i >= 2:
                        act.wait_ge(pv_done, HEADS * l + i - 1)
                    act.activation(probs_T[:, i % 2, :], bank[2 + i % 2][:, 0:KEYS], ACT.Copy).then_inc(probsT_ready, 1)

                def take_o(p):
                    act.wait_ge(pv_done, HEADS * l + 2 * p + 2)
                    act.activation(x_hi[:, p, :], bank[6 + p % 2][:, 0:S], ACT.Copy).then_inc(o_hi_ready, 1)

                for i in range(HEADS + 2):
                    if i < HEADS:
                        exps(i)
                    if 1 <= i <= HEADS:
                        take_probs(i - 1)
                    if i >= 2 and i % 2 == 1:
                        take_o((i - 2) // 2)

            for l in range(LAYERS):
                plan = PLAN[l]
                split_to(plan["in"] + AHEAD - 1)
                norm(3 * l)
                for dst, name in ((mask_bias, "mask_bias"), (head_gain, "head_gain"), (keysT, "keysT")):
                    act.dma_start(dst, a[name][l]).then_inc(layer_loaded, 16)
                if l == 0:
                    rope_tables()
                for i, b in enumerate(IN_ORDER[l]):
                    w = min(512, IN_WIDTH[l] - 512 * b)
                    take_block(plan["in"] + 4 * i, i, w, lambda t: qkv[:, t, 512 * b:512 * b + w], ACT.Copy)
                    if l == 0 and i == 1:
                        for t in range(NT):
                            act.wait_ge(idx_turned, t + 1)
                            act.activation(idxT[:, :, P * t:P * t + P],
                                           bank[6 + t][:, 0:3 * P].rearrange("p (a t) -> p a t", a=3),
                                           ACT.Copy).then_inc(idxT_ready, 1)
                    if i in (2 - l, 4 - l):
                        act.wait_ge(proj_taken, TAKEN[l] + 2 * (i + 1))
                        square_run(l, (i - 1) // 2)
                    if i == 4 - l:
                        root_run(l, 0)
                root_run(l, 1)
                for p in range(PAIRS):
                    act.wait_ge(qk_turned, PAIRS * l + p + 1)
                    act.activation(qkT[:, p, :, :].rearrange("p k t -> p (k t)"), bank[4 + p % 2][:, :],
                                   ACT.Copy).then_inc(qkT_ready, 1)
                heads(l)
                split_to(plan["query"] + AHEAD - 1)
                norm(3 * l + 1)
                for i in range(HC):
                    split_to(plan["query"] + i + AHEAD)
                    multiplied(plan["query"] + i)
                    act.activation(qryT[:, i, :], bank[4 + i % 4][:, 0:S], ACT.Copy).then_inc(qryT_ready, 1)
                for g in range(4):
                    act.wait_ge(keys_scored, 8 * l + g + 1)
                    act.activation(key_s[:, 4 * g:4 * g + 4, :].rearrange("p a k -> p (a k)"), bank[4 + g][:, :],
                                   ACT.Copy).then_inc(key_s_ready, 1)

                def gelu_half(half):
                    with act.Fori(0, J_HALF // SLOTS) as k:
                        for c in range(SLOTS):
                            j = J_HALF * half + c
                            multiplied(plan["u"] + j, k)
                            act.activation(act_ijt[:, bass.ds(k * SLOTS + j, 1), :].rearrange("p a t -> p (a t)"),
                                           bank[4 + c % 2][:, 0:S], ACT.Gelu_apprx_tanh).then_inc(gelu_done, 1)
                            split_hi(plan["u"] + j + AHEAD, k)
                    split[0] += J_HALF

                gelu_half(0)
                for t in range(NT):
                    act.wait_ge(cand_ready, 2 * l + t + 1)
                    act.activation(e_g[:, t, :, :], cv[:, t, :, :], ACT.Exp).then_inc(gexp_done, 1)
                act.wait_ge(sel_turned, 2 * (l + 1))
                gelu_half(1)

                for half in range(2):
                    act.wait_ge(gated_done, S // 4 * (2 * l + half + 1) + 2)
                    with act.Fori(0, J_HALF // SLOTS) as k:
                        for c in range(SLOTS):
                            j = J_HALF * half + c
                            multiplied(plan["v"] + j - 2, k)
                            act.activation(g_hi[:, c % 2, :], act_ijt[:, bass.ds(k * SLOTS + j, 1), :]
                                           .rearrange("p a t -> p (a t)"), ACT.Copy).then_inc(g_hi_ready, 1)
                            split_hi(plan["v"] + j + AHEAD, k)
                    split[0] += J_HALF
                norm(3 * l + 2)
                for i in range(2):
                    take_block(plan["gate"] + 4 * i, i, 512, lambda t: sig[:, t, 512 * i:512 * i + 512], ACT.Sigmoid)
                split_to(plan["up"] + 3)

        @block.vector
        def _(dve):
            steps = [0]

            def link(ins):
                steps[0] += 1
                ins.then_inc(dve_step, 1)
                dve.wait_ge(dve_step, steps[0])

            def multiplied(c):
                dve.wait_ge(piece_used, c + 1 + SLOTS)

            dve.sem_inc(gated_done, 2)
            dve.wait_ge(const_loaded, 16 * CONSTS)
            link(dve.tensor_copy(iota_bf[:], iota[:]))

            def rope_tables():
                link(dve.tensor_copy(pos_f[:], pos_i[:]))
                for t in range(NT):
                    ins = dve.tensor_scalar(rope_a[:, 2, t, :], inv_freq[:], pos_f[:, t:t + 1], None, ALU.mult)
                link(ins)
                for i in range(2):
                    src = rope_a[:, 2, :, :]
                    link(dve.tensor_scalar(rope_a[:, 3, :, :], src, 1.0 / (2 * np.pi), 0.25 * i, ALU.mult, ALU.add))
                    link(dve.tensor_scalar(rope_a[:, 3, :, :], rope_a[:, 3, :, :], ROUND, -ROUND, ALU.add, ALU.add))
                    for part in TWO_PI_PARTS:
                        link(dve.scalar_tensor_tensor(rope_a[:, i, :, :], rope_a[:, 3, :, :], -part, src, ALU.mult, ALU.add))
                        src = rope_a[:, i, :, :]
                    if i:
                        link(dve.tensor_scalar(src, src, np.pi / 2, None, ALU.add))
                    link(dve.tensor_scalar(src, src, 3.1415925, -3.1415925, ALU.min, ALU.max))
                dve.sem_inc(angle_ready, 1)
                dve.wait_ge(rope_ready, 1)
                dve.tensor_scalar(rope_sin[:, :, 0:HALF], rope_sin[:, :, HALF:ROT], -1.0, None, ALU.mult)
                link(dve.tensor_copy(rope_cos[:, :, HALF:ROT], rope_cos[:, :, 0:HALF]))

            def norm(n):
                dve.wait_ge(sumsq_done, 2 * (n + 1))
                link(dve.tensor_scalar(sumsq[:], sumsq[:], 1.0 / D, EPS, ALU.mult, ALU.add))
                dve.reciprocal(inv_var[:], sumsq[:]).then_inc(var_ready, 1)
                dve.wait_ge(rstd_ready, n + 1)
                for t in range(NT):
                    dve.tensor_scalar(xs[:, t, :], h[:, t, :], rstd[:, t:t + 1], None, ALU.mult).then_inc(xs_ready, 1)
                for c in range(NC):
                    dve.wait_ge(x_hi_ready, NC * n + 2 * (c // 2) + 2)
                    dve.scalar_tensor_tensor(x_lo[:, c, :], bank[4 + c // 2][:, S * (c % 2):S * (c % 2) + S],
                                             gain[:, n * NC + c:n * NC + c + 1], x_hi_f[:, c, :], ALU.mult,
                                             ALU.subtract).then_inc(x_lo_ready, 1)

            def rope(x, n, t):
                def table(v):
                    return v.unsqueeze(1).broadcast_to([P, n, v.shape[-1]])
                dve.tensor_tensor(rope_t[:, 0, 0:n, :], x[:, :, 0:ROT], table(rope_cos[:, t, :]), ALU.mult)
                dve.tensor_tensor(rope_t[:, 1, 0:n, 0:HALF], x[:, :, HALF:ROT], table(rope_sin[:, t, 0:HALF]), ALU.mult)
                link(dve.tensor_tensor(rope_t[:, 1, 0:n, HALF:ROT], x[:, :, 0:HALF], table(rope_sin[:, t, HALF:ROT]), ALU.mult))
                return dve.tensor_tensor(x[:, :, 0:ROT], rope_t[:, 0, 0:n, :], rope_t[:, 1, 0:n, :], ALU.add)

            def var_run(l, r):
                for t in range(NT):
                    u = 2 * r + t
                    dve.wait_ge(qk_squared, 4 * l + u + 1)
                    ins = dve.tensor_reduce(h_sumsq[:, u, :], squares[:, u, :, :], AX_X, ALU.add)
                link(ins)
                v = h_sumsq[:, 2 * r:2 * r + 2, :]
                link(dve.tensor_scalar(v, v, 1.0 / DH, EPS, ALU.mult, ALU.add))
                dve.reciprocal(h_inv_var[:, 2 * r:2 * r + 2, :], v).then_inc(h_var_ready, 1)

            def norm_run(l, r):
                dve.wait_ge(h_rstd_ready, 2 * l + r + 1)
                for t in range(NT):
                    u, c = 2 * r + t, QK_RUN[l][r]
                    x = qkv[:, t, c:c + HEADS * DH].rearrange("p (n d) -> p n d", d=DH)
                    link(dve.tensor_tensor(x, x, h_rstd[:, u, :].unsqueeze(2).broadcast_to([P, HEADS, DH]), ALU.mult))
                    x4 = x.rearrange("p (b n) d -> p b n d", b=2)
                    link(dve.tensor_tensor(x4, x4, head_gain[:, r, :, :].unsqueeze(2).broadcast_to([P, 2, 8, DH]),
                                           ALU.mult))
                    rope(x, HEADS, t).then_inc(qk_ready, 1)

            def rope_indexer():
                dve.wait_ge(proj_taken, NT)
                for t in range(NT):
                    x = qkv[:, t, IDX_COL:WI_COL].rearrange("p (n d) -> p n d", d=DH)
                    link(rope(x, IDX_HEADS + 1, t))
                    dve.tensor_copy(kk[:, t, :].rearrange("p (b d) -> p b d", b=2),
                                    x[:, IDX_HEADS:IDX_HEADS + 1, :].broadcast_to([P, 2, DH])).then_inc(idx_ready, 1)

            def index_scores():
                for t, (x, y) in enumerate(SEG):
                    dve.wait_ge(logits_done, t + 1)
                    for i in range(IDX_HEADS):
                        src = bank[6][:, P * i:P * i + P] if t == 0 else bank[4 + i // 2][:, S * (i % 2):S * (i % 2) + S]
                        dst = idx_r if i else idx_s
                        link(dve.tensor_scalar(dst[:, x:y], src, 0.0, qkv[:, t, WI_COL + i:WI_COL + i + 1], ALU.max, ALU.mult))
                        if i:
                            link(dve.tensor_tensor(idx_s[:, x:y], idx_s[:, x:y], idx_r[:, x:y], ALU.add))
                dve.tensor_tensor(idx_s[:], idx_s[:], mask_bias[:], ALU.add).then_inc(logits_taken, 1)
                dve.wait_ge(logits_taken, 1)

            def select_dsa(t):
                x, y = SEG[t]
                for _ in range(DSA_TOPK // 8):
                    link(dve.max(out=top8[:], in_=idx_s[:, x:y]))
                    link(dve.match_replace(out=idx_s[:, x:y], in_to_replace=top8[:], in_values=idx_s[:, x:y], imm_value=GONE))
                link(dve.tensor_scalar(idx_r[:, x:y], idx_s[:, x:y], GONE / 2, NEG, ALU.is_gt, ALU.mult))
                link(dve.tensor_tensor(bias_dsa[:, x:y], idx_r[:, x:y], mask_bias[:, x:y], ALU.add))

            def heads(l):
                def bias(i):
                    mask = bias_dsa if l == 0 and i >= 8 else mask_bias
                    dve.wait_ge(scores_done, HEADS * l + i + 1)
                    if i >= 2:
                        dve.wait_ge(exp_done, 2 * (HEADS * l + i - 1))
                    dve.scalar_tensor_tensor(biased[:, i % 2, :], bank[i % 2][:, 0:KEYS], SCALE, mask[:, :], ALU.mult,
                                             ALU.add).then_inc(biased_ready, 1)
                    dve.wait_ge(biased_ready, HEADS * l + i + 1)
                    for t, (x, y) in enumerate(SEG):
                        dve.tensor_reduce(neg_max[:, i % 2, t:t + 1], biased[:, i % 2, x:y], AX_X, ALU.max,
                                          negate=True).then_inc(negmax_ready, 1)

                def scale(i):
                    dve.wait_ge(exp_done, 2 * (HEADS * l + i + 1))
                    if i >= 2:
                        dve.wait_ge(probs_turned, HEADS * l + i - 1)
                    link(dve.reciprocal(inv_denom[:, i % 2, :], denom[:, i % 2, :]))
                    for t, (x, y) in enumerate(SEG):
                        dve.tensor_scalar(probs_n[:, i % 2, x:y], probs[:, i % 2, x:y], inv_denom[:, i % 2, t:t + 1], None,
                                          ALU.mult).then_inc(probs_ready, 1)

                def take_o(p):
                    dve.wait_ge(o_hi_ready, PAIRS * l + p + 1)
                    dve.tensor_tensor(x_lo[:, p, :], bank[6 + p % 2][:, 0:S], x_hi_f[:, p, :], ALU.subtract).then_inc(o_lo_ready, 1)

                for i in range(HEADS + 3):
                    if i < HEADS:
                        bias(i)
                    if 1 <= i <= HEADS:
                        scale(i - 1)
                    if i >= 4 and i % 2 == 0:
                        take_o((i - 4) // 2)

            def add_blocks(l, kind):
                for b in range(2):
                    multiplied(PLAN[l]["out"] + 4 * b + 3 if kind == "out" else PLAN[l]["up"] + 2 * b + 1)
                    for t in range(NT):
                        x = h[:, t, 512 * b:512 * b + 512]
                        y = bank[2 * b + t][:, :]
                        if kind == "up":
                            gate = sig[:, t, 512 * b:512 * b + 512]
                            link(dve.tensor_tensor(gate, y, gate, ALU.mult))
                            y = gate
                        dve.tensor_tensor(x, x, y, ALU.add).then_inc(h_written, 1)

            def top16(values, indices, src):
                link(dve.max(out=values[:, 0:8], in_=src))
                dve.max_index(out=indices[:, 0:8], in_max=values[:, 0:8], in_values=src)
                link(dve.match_replace(out=src, in_to_replace=values[:, 0:8], in_values=src, imm_value=GONE))
                link(dve.max(out=values[:, 8:16], in_=src))
                return dve.max_index(out=indices[:, 8:16], in_max=values[:, 8:16], in_values=src)

            def select_experts(l):
                for t in range(NT):
                    for n in range(HC):
                        if t == 0:
                            dve.wait_ge(key_s_ready, 4 * l + n // 4 + 1)
                            src = key_s[:, n, :]
                        else:
                            dve.wait_ge(keys_scored, 8 * l + 4 + n // 4 + 1)
                            src = bank[n // 4][:, NK * (n % 4):NK * (n % 4) + NK]
                        ins = top16(sv[:, n, :], si[:, n, :], src)
                    link(ins)
                    halves = sv[:, :, :].rearrange("p (g c) k -> p g c k", c=2)
                    link(dve.tensor_tensor(cand, halves[:, :, 0, :].unsqueeze(3).broadcast_to([P, PH, TOPK, TOPK]),
                                           halves[:, :, 1, :].unsqueeze(2).broadcast_to([P, PH, TOPK, TOPK]), ALU.add))
                    dve.tensor_copy(si_f, si)
                    for g in range(PH):
                        ins = top16(cv[:, t, g, :], ci[:, g, :], cand[:, g, :, :].rearrange("p a b -> p (a b)"))
                    link(ins)
                    dve.tensor_scalar(rank[:, 0, :, :], ci, 4, None, ALU.logical_shift_right)
                    link(dve.tensor_scalar(rank[:, 1, :, :], ci, 15, None, ALU.bitwise_and))
                    link(dve.tensor_copy(rank_f, rank))
                    idx = si_f[:, :, :].rearrange("p (g c) k -> p g c k", c=2)
                    for c, e in enumerate((e_i, e_j)):
                        link(dve.tensor_tensor(eq, rank_f[:, c, :, :].unsqueeze(3).broadcast_to([P, PH, TOPK, TOPK]),
                                               iota[:, 0:TOPK].unsqueeze(1).unsqueeze(1).broadcast_to([P, PH, TOPK, TOPK]),
                                               ALU.is_equal))
                        link(dve.tensor_tensor(eq, eq, idx[:, :, c, :].unsqueeze(2).broadcast_to([P, PH, TOPK, TOPK]), ALU.mult))
                        link(dve.tensor_reduce(e[:, t, :, :], eq, AX_X, ALU.add))
                    link(dve.tensor_reduce(g_inv[:, t, :], cv[:, t, :, :], AX_X, ALU.max))
                    dve.tensor_tensor(cv[:, t, :, :], cv[:, t, :, :], g_inv[:, t, :].unsqueeze(2).broadcast_to([P, PH, TOPK]),
                                      ALU.subtract).then_inc(cand_ready, 1)
                for t in range(NT):
                    dve.wait_ge(gexp_done, 2 * l + t + 1)
                    link(dve.tensor_reduce(g_sum[:, t, :], e_g[:, t, :, :], AX_X, ALU.add))
                    link(dve.reciprocal(g_inv[:, t, :], g_sum[:, t, :]))
                    dve.tensor_tensor(e_g[:, t, :, :], e_g[:, t, :, :], g_inv[:, t, :].unsqueeze(2).broadcast_to([P, PH, TOPK]),
                                      ALU.mult).then_inc(sel_ready, 1)
                for t in range(NT):
                    dve.wait_ge(sel_turned, 2 * l + t + 1)
                    tok = slice(P * t, P * t + P)
                    dve.tensor_copy(ijT[:, :, tok], bank[6 + t][:, 0:2 * P].rearrange("p (e t) -> p e t", e=2))
                    src = bank[6 + t][:, 2 * P:3 * P]
                    link(dve.tensor_copy(gT[:, 0, tok], src))
                    for i in range(2):
                        link(dve.tensor_tensor(g_rest[:, i, tok], src, gT[:, i, tok], ALU.subtract))
                        src = g_rest[:, i, tok]
                        link(dve.tensor_copy(gT[:, i + 1, tok], src))

            def gate_group(l, half, c, k, lag=True):
                n = S // 4 * (2 * l + half) + c
                dve.wait_ge(gates_done, n + k * SLOTS + 1)
                tok = bass.ds(k * (4 * SLOTS) + 4 * c, 4)
                dve.tensor_tensor(hot_j[:, c % 2, :, :], iota_bf[:, J_HALF * half:J_HALF * half + J_HALF].unsqueeze(1)
                                  .broadcast_to([P, 4, J_HALF]), ijT[:, 1, tok].unsqueeze(2).broadcast_to([P, 4, J_HALF]),
                                  ALU.is_equal).then_inc(hot_j_ready, 1)
                dve.tensor_tensor(hot_i[:, c % 2, :, :], iota_bf[:, :].unsqueeze(1).broadcast_to([P, 4, P]),
                                  ijT[:, 0, tok].unsqueeze(2).broadcast_to([P, 4, P]), ALU.is_equal)
                dve.wait_ge(hot_j_ready, n + k * SLOTS + 1)
                dve.tensor_tensor(hot_jg[:, c % 2, :, :, :], hot_j[:, c % 2, :, :].unsqueeze(1).broadcast_to([P, 3, 4, J_HALF]),
                                  gT[:, :, tok].unsqueeze(3).broadcast_to([P, 3, 4, J_HALF]), ALU.mult).then_inc(hot_ready, 1)
                if lag:
                    gated(l, half, c - 1, k)

            def gated(l, half, c, k):
                n = S // 4 * (2 * l + half) + c
                tok = bass.ds(k * (4 * SLOTS) + 4 * c, 4)
                dve.wait_ge(gates_done, n + k * SLOTS + 3)
                x = act_itj[:, tok, J_HALF * half:J_HALF * half + J_HALF]
                dve.tensor_tensor(x, x, bank[6 + c % 2][:, 0:4 * J_HALF].rearrange("p (q j) -> p q j", q=4),
                                  ALU.mult).then_inc(gated_done, 1)

            def gated_lo(l, j, k):
                dve.wait_ge(g_hi_ready, NK * l + k * SLOTS + j + 1)
                dve.tensor_tensor(g_lo[:, j % 2, :], act_ijt[:, bass.ds(k * SLOTS + j, 1), :].rearrange("p a t -> p (a t)"),
                                  g_hi_f[:, j % 2, :], ALU.subtract).then_inc(g_lo_ready, 1)

            def gate_experts(l):
                quarter = J_HALF // SLOTS
                dve.wait_ge(gelu_done, NK * l + J_HALF + 2)
                for c in range(SLOTS):
                    gate_group(l, 0, c, 0, c > 0)
                with dve.Fori(1, quarter) as k:
                    for c in range(SLOTS):
                        gate_group(l, 0, c, k)
                gated(l, 0, J_HALF - 1, 0)
                dve.wait_ge(gelu_done, NK * (l + 1) + 2)
                for c in range(SLOTS):
                    gated_lo(l, c, 0)
                    gate_group(l, 1, c, 0, c > 0)
                with dve.Fori(1, quarter) as k:
                    for c in range(SLOTS):
                        gated_lo(l, c, k)
                        gate_group(l, 1, c, k)
                gated(l, 1, J_HALF - 1, 0)
                with dve.Fori(0, quarter) as k:
                    for c in range(SLOTS):
                        gated_lo(l, J_HALF + c, k)

            for l in range(LAYERS):
                norm(3 * l)
                dve.wait_ge(layer_loaded, 48 * (l + 1))
                if l == 0:
                    rope_tables()
                    rope_indexer()
                    index_scores()
                    select_dsa(0)
                    var_run(l, 0)
                    select_dsa(1)
                else:
                    var_run(l, 0)
                norm_run(l, 0)
                var_run(l, 1)
                norm_run(l, 1)
                heads(l)
                add_blocks(l, "out")
                norm(3 * l + 1)
                select_experts(l)
                gate_experts(l)
                multiplied(PLAN[l]["v"] + NK - 1)
                for t in range(NT):
                    for b in range(2):
                        x = h[:, t, 512 * b:512 * b + 512]
                        dve.tensor_tensor(x, x, bank[2 * t + b][:, :], ALU.add).then_inc(h_written, 1)
                norm(3 * l + 2)
                dve.wait_ge(proj_taken, TAKEN[l] + 2 * len(IN_ORDER[l]) + 4)
                add_blocks(l, "up")


def by_blocks(w, order):
    for b in order:
        block = w[:, 512 * b:512 * b + 512]
        yield np.pad(block, ((0, 0), (0, 512 - block.shape[1]))).reshape(4, 2, P, 512).transpose(0, 2, 1, 3)


def by_columns(w):
    return w.reshape(NC, P, -1, P).transpose(2, 1, 0, 3)


def weight_stream(i):
    stream = np.empty((PIECES, P, PIECE), np.float32)
    at = 0

    def put(pieces):
        nonlocal at
        n = len(pieces)
        stream[at:at + n].reshape((n, *pieces.shape[1:]))[...] = pieces
        at += n

    for l, (w_in, w_out) in enumerate((("ab_w_in", "ab_w_out"), ("c_w_in", "c_w_out"))):
        for pieces in by_blocks(i[w_in][0], IN_ORDER[l]):
            put(pieces)
        for pieces in by_blocks(i[w_out][0], range(2)):
            put(pieces)
        put(by_columns(i["peer_w_query"][l]))
        put(i["peer_u"][l].reshape(NK, NK, NC, P).transpose(1, 3, 2, 0))
        put(i["peer_v"][l].reshape(NK, NK, D).transpose(1, 0, 2))
        for pieces in by_blocks(i["ple_w_gate"][l], range(2)):
            put(pieces)
        emb = i["p"][l, 0].T.reshape(2, P, S).transpose(1, 0, 2)
        up = i["ple_w_up"][l].reshape(2, P, 4, S).transpose(2, 1, 0, 3)
        put(np.stack([np.concatenate([emb, u], axis=2) for u in up]))
    assert at == PIECES
    return stream


def shape_constants():
    t = np.arange(P)[:, None]
    causal, dilated = [], []
    for tile, (x, y) in enumerate(SEG):
        dist = t + P * tile - np.arange(y - x)[None, :]
        count = np.zeros(dist.shape, np.int64)
        for window, dil in ((128, 1), (512, 4), (2048, 16)):
            count += (dist >= 0) & (dist <= window) & (dist % dil == 0)
        causal.append(np.where(dist >= 0, 0.0, NEG))
        dilated.append(np.where(count > 0, np.log(np.maximum(count, 1)), NEG))
    half = np.arange(HALF, dtype=np.float32)
    inv = np.power(np.float32(500000.0), -half / np.float32(HALF)).astype(np.float32)
    return {
        "ident": np.eye(P, dtype=np.float32),
        "iota": np.tile(np.arange(P, dtype=np.float32), (P, 1)),
        "mask_bias": np.stack([np.concatenate(v, axis=1) for v in (causal, dilated)]).astype(np.float32),
        "inv_freq": np.tile(inv, (P, 1)),
    }


def lay_out(i):
    a = shape_constants()
    c = np.ascontiguousarray
    a["x"] = c(i["x"][0])
    a["positions"] = c(i["positions"][0].reshape(NT, P).T)
    gains = np.stack([i[n][l] for l in range(LAYERS) for n in ("attn_norm", "ffn_norm", "ple_norm")])
    a["gain"] = c(gains.reshape(3 * LAYERS * NC, P).T)
    hg = np.stack([i["a_q_norm"][0], i["a_k_norm"][0], i["b_q_norm"][0], i["b_k_norm"][0],
                   i["c_q_norm"][0], i["c_q_norm"][0], i["c_k_norm"][0], i["c_k_norm"][0]])
    a["head_gain"] = c(np.broadcast_to(hg.reshape(LAYERS, 1, 2, 2, DH), (LAYERS, P, 2, 2, DH)))
    a["keysT"] = c(i["peer_sub_keys"].reshape(LAYERS, HC, NK, P).transpose(0, 3, 1, 2))
    a["stream"] = weight_stream(i)
    return a


def kernel(**inputs):
    import concourse.bacc as bacc
    from concourse.bass_utils import run_bass_kernel_spmd

    arrays = lay_out({k: np.asarray(v) for k, v in inputs.items()})
    nc = bacc.Bacc("TRN2", target_bir_lowering=False, num_devices=1)
    aps = {k: nc.dram_tensor(f"in_{k}", v.shape, mybir.dt.from_np(v.dtype), kind="ExternalInput").ap()
           for k, v in arrays.items()}
    out = nc.dram_tensor("out", (S, D), F32, kind="ExternalOutput").ap()
    hybrid_trunk(nc, aps, out)
    r = run_bass_kernel_spmd(nc, [{f"in_{k}": v for k, v in arrays.items()}], core_ids=[0])
    return r.results[0]["out"].reshape(1, S, D)
```

```python
from contextlib import ExitStack

import numpy as np

import concourse.bass as bass
from concourse import mybir

ALU = mybir.AluOpType
ACT = mybir.ActivationFunctionType
F32 = mybir.dt.float32
F32R = mybir.dt.float32r
BF16 = mybir.dt.bfloat16
U32 = mybir.dt.uint32
I32 = mybir.dt.int32
AX_X = mybir.AxisListType.X

P = 128
D = 1024
S = 256
NT = S // P
NC = D // P
LAYERS = 2
DH = 64
ROT = 16
HALF = ROT // 2
EPS = 1e-6
NEG = -1e30
GONE = -3e38
HEADS = 16
PAIRS = HEADS // 2
IN_WIDTH = (3396, 3072)
V_COL = ([1024 + DH * h for h in range(8)] + [2560 + DH * h for h in range(8)],
         [2048 + DH * h for h in range(16)])
QK_RUN = ((0, 1536), (0, 1024))
Q_COL = ([128 * p for p in range(4)] + [1536 + 128 * p for p in range(4)], [128 * p for p in range(8)])
K_COL = ([512 + 128 * p for p in range(4)] + [2048 + 128 * p for p in range(4)],
         [1024 + 128 * p for p in range(8)])
IDX_COL, IDX_HEADS, WI_COL = 3072, 4, 3392
DSA_TOPK = 64
PH = 8
HC = 2 * PH
NK = 128
TOPK = 16
KEYS = P + 2 * P
SEG = ((0, P), (P, 3 * P))
SCALE = DH ** -0.5
TWO_PI_PARTS = (6.28125, 1.9350051879882812e-03, 3.0199159819567529e-07)
ROUND = 12582912.0

PIECE = 1024
SLOTS = 4
LO_SLOTS = 2
AHEAD = 3
G_SLOTS = 4
J_EXP, J_TURN = 44, 52
J_HALF = NK // 2
IN_ORDER = ([6, 0, 1, 3, 4, 2, 5], [0, 1, 2, 3, 4, 5])


def stream_plan():
    plan, at = [], 0
    for l in range(LAYERS):
        part = {}
        for kind, n in (("in", 4 * len(IN_ORDER[l])), ("out", 8), ("query", HC), ("u", NK), ("v", NK),
                        ("up", 4), ("gate", 8)):
            part[kind] = at
            at += n
        plan.append(part)
    return plan, at


PLAN, PIECES = stream_plan()
assert PIECES % SLOTS == 0 and all(v % SLOTS == 0 for part in PLAN for v in part.values())
BLOCKS = [[(0, 0), (1, 0), (0, 1), (1, 1)], [(0, 0), (1, 0), (0, 1), (1, 1)], [(0, 0), (0, 1), (1, 0), (1, 1)]]
TURN_BANK = [4, 4, 0]
TAKEN = [0, 2 * (len(IN_ORDER[0]) + 2)]


def hybrid_trunk(nc, a, out):
    with ExitStack() as ctx:
        def sb(name, shape, dt=F32):
            return ctx.enter_context(nc.sbuf_tensor(name, shape, dt))

        def sem(name):
            return ctx.enter_context(nc.semaphore(name))

        h = sb("h", [P, NT, D])
        x_hi = sb("x_hi", [P, NC, S], F32R)
        x_lo = sb("x_lo", [P, NC, S], F32R)
        raw = sb("raw", [P, SLOTS, PIECE])
        w_hi = sb("w_hi", [P, SLOTS, PIECE], F32R)
        w_lo = sb("w_lo", [P, LO_SLOTS, PIECE], F32R)
        arena = sb("arena", [P, P * S])
        hot_i = sb("hot_i", [P, 2, 4, P], BF16)
        hot_j = sb("hot_j", [P, 2, 4, J_HALF], BF16)
        hot_jg = sb("hot_jg", [P, 2, 3, 4, J_HALF], BF16)
        ident = sb("ident", [P, P])
        iota = sb("iota", [P, P])
        iota_bf = sb("iota_bf", [P, P], BF16)
        gain = sb("gain", [P, 3 * LAYERS * NC])
        inv_freq = sb("inv_freq", [P, HALF])
        pos_i = sb("pos_i", [P, NT], I32)
        pos_f = sb("pos_f", [P, NT])
        rope_a = sb("rope_a", [P, 4, NT, HALF])
        rope_cos = sb("rope_cos", [P, NT, ROT])
        rope_sin = sb("rope_sin", [P, NT, ROT])
        sumsq = sb("sumsq", [P, NT, 2])
        mean_sq = sb("mean_sq", [P, NT])
        inv_var = sb("inv_var", [P, NT])
        rstd = sb("rstd", [P, NT])
        table_load = sb("table_load", [P, 3 * LAYERS])
        h_sumsq = sb("h_sumsq", [P, 2 * NT, HEADS])
        h_inv_var = sb("h_inv_var", [P, 2 * NT, HEADS])
        h_rstd = sb("h_rstd", [P, 2 * NT, HEADS])
        top8 = sb("top8", [P, 8])
        neg_max = sb("neg_max", [P, 2, NT])
        denom = sb("denom", [P, 2, NT])
        inv_denom = sb("inv_denom", [P, 2, NT])
        cv = sb("cv", [P, NT, PH, TOPK])
        e_g = sb("e_g", [P, NT, PH, TOPK])
        g_sum = sb("g_sum", [P, NT, PH])
        g_inv = sb("g_inv", [P, NT, PH])
        ijT = sb("ijT", [P, 2, S], BF16)
        gT = sb("gT", [P, 3, S], BF16)
        g_rest = sb("g_rest", [P, 2, S])

        x_hi_f, w_hi_f = (v.bitcast(F32) for v in (x_hi[:, :, :], w_hi[:, :, :]))
        g_hi, g_lo, g_hi_f = (v[:, 0:G_SLOTS, :] for v in (x_hi, x_lo, x_hi_f))

        at = [0]

        def region(*shape, dt=F32):
            n = int(np.prod(shape))
            at[0] += n
            assert at[0] <= P * S
            v = arena[:, at[0] - n:at[0]]
            v = v if dt is F32 else v.bitcast(dt)
            names = "abcd"[:len(shape)]
            return v.rearrange(f"p ({' '.join(names)}) -> p {' '.join(names)}", **dict(zip(names, shape)))

        xs = region(NT, D)
        qkv = region(NT, IN_WIDTH[0])
        sig = region(NT, D)
        kk = region(NT, P)
        idxT = region(3, S)
        idx_s = region(KEYS)
        idx_r = region(KEYS)
        bias_dsa = region(KEYS)
        rope_t = region(2, HEADS, ROT)
        mask_bias = region(KEYS)
        head_gain = region(2, 2, DH)
        at[0] = max(at[0], J_HALF * S)
        upper = at[0]
        qkT = region(PAIRS, 2, S)
        squares = region(2 * NT, HEADS, DH)
        biased = region(2, KEYS)
        probs = region(2, KEYS)
        probs_n = region(2, KEYS)
        probs_T = region(4, KEYS)
        at[0] = upper
        qryT = region(HC, S)
        key_s = region(HC, NK)
        cand = region(PH, TOPK, TOPK)
        eq = region(PH, TOPK, TOPK)
        sv = region(HC, TOPK)
        si = region(HC, TOPK, dt=U32)
        si_f = region(HC, TOPK)
        ci = region(PH, TOPK, dt=U32)
        rank = region(2, PH, TOPK, dt=U32)
        rank_f = region(2, PH, TOPK)
        e_i = region(NT, PH, TOPK)
        e_j = region(NT, PH, TOPK)
        keysT = region(HC, NK)
        act_ijt = arena[:, :].rearrange("p (j t) -> p j t", t=S)
        act_itj = arena[:, :].rearrange("p (j t) -> p t j", t=S)

        bank = [ctx.enter_context(nc.psum_tensor(f"bank{i}", [P, 512], F32)) for i in range(8)]

        const_loaded = sem("const_loaded")
        ident_loaded = sem("ident_loaded")
        h_loaded = [sem(f"h_loaded{t}") for t in range(NT)]
        angle_ready = sem("angle_ready")
        rope_ready = sem("rope_ready")
        piece_loaded = [sem(f"piece_loaded{i}") for i in range(SLOTS)]
        hi_ready = sem("hi_ready")
        lo_ready = sem("lo_ready")
        piece_used = sem("piece_used")
        tile_done = sem("tile_done")
        layer_loaded = sem("layer_loaded")
        stored = sem("stored")
        sumsq_done = sem("sumsq_done")
        var_ready = sem("var_ready")
        rstd_ready = sem("rstd_ready")
        xs_ready = sem("xs_ready")
        xs_turned = sem("xs_turned")
        x_hi_ready = sem("x_hi_ready")
        x_lo_ready = sem("x_lo_ready")
        proj_taken = sem("proj_taken")
        h_written = sem("h_written")
        qk_squared = sem("qk_squared")
        h_var_ready = sem("h_var_ready")
        h_rstd_ready = sem("h_rstd_ready")
        qk_ready = sem("qk_ready")
        idx_ready = sem("idx_ready")
        qk_turned = sem("qk_turned")
        qkT_ready = sem("qkT_ready")
        idx_turned = sem("idx_turned")
        idxT_ready = sem("idxT_ready")
        even_logits = sem("even_logits")
        logits_done = sem("logits_done")
        logits_taken = sem("logits_taken")
        scores_done = sem("scores_done")
        biased_ready = sem("biased_ready")
        negmax_ready = sem("negmax_ready")
        exp_done = sem("exp_done")
        probs_ready = sem("probs_ready")
        probs_turned = sem("probs_turned")
        probsT_ready = sem("probsT_ready")
        pv_done = sem("pv_done")
        o_hi_ready = sem("o_hi_ready")
        o_lo_ready = sem("o_lo_ready")
        qryT_ready = sem("qryT_ready")
        keys_scored = sem("keys_scored")
        key_s_ready = sem("key_s_ready")
        gelu_done = sem("gelu_done")
        cand_ready = sem("cand_ready")
        gexp_done = sem("gexp_done")
        sel_ready = sem("sel_ready")
        sel_turned = sem("sel_turned")
        hot_j_ready = sem("hot_j_ready")
        hot_ready = sem("hot_ready")
        gates_done = sem("gates_done")
        gated_done = sem("gated_done")
        g_hi_ready = sem("g_hi_ready")
        g_lo_ready = sem("g_lo_ready")
        dve_step = sem("dve_step")

        block = ctx.enter_context(nc.Block())
        CONSTS = 3


        @block.sync
        def _(sp):
            for dst, src in ((ident[:], a["ident"]), (gain[:], a["gain"])):
                sp.dma_start(dst, src).then_inc(ident_loaded, 16)
            for i in range(NT):
                sp.dma_start(h[:, i, :], a["x"][P * i:P * i + P, :]).then_inc(h_loaded[i], 16)
            for dst, src in ((inv_freq[:], a["inv_freq"]), (pos_i[:], a["positions"]), (iota[:], a["iota"])):
                sp.dma_start(dst, src).then_inc(const_loaded, 16)
            with sp.Fori(0, PIECES // SLOTS) as k:
                for c in range(SLOTS):
                    sp.wait_ge(hi_ready, k * SLOTS + c + 1)
                    sp.wait_ge(lo_ready, k * SLOTS + c + 1)
                    sp.dma_start(raw[:, c, :], a["stream"][bass.ds(k * SLOTS + c, 1), :, :]
                                 .rearrange("a p n -> (a p) n")).then_inc(piece_loaded[c], 16)
            for u, (t, b) in enumerate(BLOCKS[0]):
                sp.wait_ge(h_written, 12 * LAYERS - 4 + u + 1)
                sp.dma_start(out[P * t:P * t + P, 512 * b:512 * b + 512],
                             h[:, t, 512 * b:512 * b + 512]).then_inc(stored, 16)
            sp.wait_ge(stored, 16 * len(BLOCKS[0]))

        @block.gpsimd
        def _(pool):
            pool.sem_inc(lo_ready, SLOTS)
            with pool.Fori(0, PIECES // SLOTS) as k:
                for c in range(SLOTS):
                    pool.wait_ge(hi_ready, k * SLOTS + c + 1 + SLOTS)
                    pool.wait_ge(piece_used, k * SLOTS + c + 1 + SLOTS - LO_SLOTS)
                    pool.tensor_tensor(w_lo[:, c % LO_SLOTS, :], raw[:, c, :], w_hi_f[:, c, :], ALU.subtract) \
                        .then_inc(lo_ready, 1)

        @block.tensor
        def _(pe):
            pe.sem_inc(piece_used, SLOTS)
            pe.sem_inc(gates_done, 2)
            pe.wait_ge(ident_loaded, 32)

            def multiply(c, k, terms, w_moves=True, ready=None, tile_first=False):
                hi, lo = w_hi[:, c % SLOTS, :], w_lo[:, c % LO_SLOTS, :]
                pe.wait_ge(hi_ready, k * SLOTS + c + 1 + SLOTS)
                half = len(terms) // 2
                for part in (terms[:half], terms[half:]) if tile_first else (terms,):
                    for n, (dst, x, cols, first, _) in enumerate(part):
                        if ready:
                            pe.wait_ge(ready[0], ready[1] + n + 1)
                        for i in range(2):
                            st, mv = (x[i], hi[:, cols]) if w_moves else (hi[:, cols], x[i])
                            pe.matmul(dst, st, mv, start=first and i == 0, stop=False)
                    pe.wait_ge(lo_ready, k * SLOTS + c + 1 + SLOTS)
                    for dst, x, cols, _, last in part:
                        st, mv = (x[0], lo[:, cols]) if w_moves else (lo[:, cols], x[0])
                        mm = pe.matmul(dst, st, mv, start=False, stop=last)
                    if tile_first and part[0] is terms[0]:
                        mm.then_inc(tile_done, 1)
                mm.then_inc(piece_used, 1)

            def turn_normed(n):
                for t in range(NT):
                    for c in range(NC):
                        if c % 4 == 0:
                            pe.wait_ge(xs_ready, 4 * n + 2 * t + c // 4 + 1)
                        q = (c % 2) * S + t * P
                        mm = pe.transpose(bank[TURN_BANK[n % 3] + c // 2][:, q:q + P], xs[:, t, c * P:c * P + P], ident[:])
                        if t == NT - 1 and c % 2:
                            mm.then_inc(xs_turned, 1)

            def project(m, i, width=512, ready=None, least=0, tile_first=False):
                for q in range(4):
                    if ready:
                        pe.wait_ge(ready[0], ready[1] + max(2 * q + 2, least))
                    multiply(m + q, 0, [(bank[2 * (i % 2) + t][:, 0:width],
                                         [v[:, 2 * q + c, P * t:P * t + P] for v in (x_hi, x_lo)],
                                         slice(512 * c, 512 * c + width), q == 0 and c == 0, q == 3 and c == 1)
                                        for t in range(NT) for c in range(2)], tile_first=tile_first and q == 3)

            def turned_project(c, k, dst, ready=None):
                multiply(c, k, [(dst, [v[:, i, :] for v in (x_hi, x_lo)], slice(P * i, P * i + P), i == 0, i == NC - 1)
                                for i in range(NC)], w_moves=False, ready=ready)

            def index_logits():
                pe.wait_ge(idx_ready, NT)
                for t in range(NT):
                    for i in range(3):
                        src = kk[:, t, :] if i == 2 else qkv[:, t, IDX_COL + P * i:IDX_COL + P * i + P]
                        mm = pe.transpose(bank[6 + t][:, P * i:P * i + P], src, ident[:])
                    mm.then_inc(idx_turned, 1)
                pe.wait_ge(idxT_ready, NT)
                for t in range(NT):
                    for i in (0, 2, 1, 3):
                        o = DH * (i % 2)
                        if i == 1:
                            mm.then_inc(even_logits, 1)
                            pe.wait_ge(even_logits, t + 1)
                        dst = bank[6][:, P * i:P * i + P] if t == 0 else bank[4 + i // 2][:, S * (i % 2):S * (i % 2) + S]
                        mm = pe.matmul(dst, idxT[o:o + DH, i // 2, P * t:P * t + P],
                                       idxT[o:o + DH, 2, 0:P * (t + 1)], start=True, stop=True)
                    mm.then_inc(logits_done, 1)

            def project_in(l):
                for i, b in enumerate(IN_ORDER[l]):
                    if i >= 2:
                        pe.wait_ge(proj_taken, TAKEN[l] + 2 * (i - 1))
                    project(PLAN[l]["in"] + 4 * i, i, min(512, IN_WIDTH[l] - 512 * b),
                            ready=(x_lo_ready, NC * 3 * l) if i == 0 else None)
                    if l == 0 and i == 1:
                        index_logits()

            def heads(l):
                def turn_qk(p):
                    pe.wait_ge(qk_ready, 4 * l + (2 * (1 + p // 4) if l == 0 else 4))
                    if p >= 2:
                        pe.wait_ge(qkT_ready, PAIRS * l + p - 1)
                    for i, col in enumerate((Q_COL[l][p], K_COL[l][p])):
                        for t in range(NT):
                            q = i * S + t * P
                            mm = pe.transpose(bank[4 + p % 2][:, q:q + P], qkv[:, t, col:col + P], ident[:])
                    mm.then_inc(qk_turned, 1)

                def scores(i):
                    o, p = DH * (i % 2), i // 2
                    pe.wait_ge(qkT_ready, PAIRS * l + p + 1)
                    if i >= 2:
                        pe.wait_ge(biased_ready, HEADS * l + i - 1)
                    for t in range(NT):
                        mm = pe.matmul(bank[i % 2][:, SEG[t][0]:SEG[t][1]], qkT[o:o + DH, p, 0, P * t:P * t + P],
                                       qkT[o:o + DH, p, 1, 0:P * (t + 1)], start=True, stop=True)
                    mm.then_inc(scores_done, 1)

                def turn(i):
                    pe.wait_ge(probs_ready, 2 * (HEADS * l + i + 1))
                    if i >= 2:
                        pe.wait_ge(probsT_ready, HEADS * l + i - 1)
                    for q in range(3):
                        mm = pe.transpose(bank[2 + i % 2][:, P * q:P * q + P], probs_n[:, i % 2, P * q:P * q + P], ident[:])
                    mm.then_inc(probs_turned, 1)

                def pv(p):
                    pe.wait_ge(probsT_ready, HEADS * l + 2 * p + 2)
                    if p >= 2:
                        pe.wait_ge(o_lo_ready, PAIRS * l + p - 1)
                    for s, (x, y) in enumerate(((0, 2 * P), (2 * P, 3 * P))):
                        for i in (2 * p, 2 * p + 1):
                            o, c = DH * (i % 2), V_COL[l][i]
                            mm = pe.matmul(bank[6 + p % 2][o:o + DH, P * s:S], qkv[:, s, c:c + DH],
                                           probs_T[:, i % 4, x:y], start=s == 0, stop=s == 1)
                    mm.then_inc(pv_done, 1)

                if l == 0:
                    pe.wait_ge(logits_taken, 1)
                turn_qk(0)
                turn_qk(1)
                pe.wait_ge(proj_taken, TAKEN[l] + 2 * len(IN_ORDER[l]))
                scores(0)
                for i in range(HEADS + 2):
                    if i + 1 < HEADS:
                        scores(i + 1)
                    if i % 2 == 0 and i // 2 + 2 < PAIRS:
                        turn_qk(i // 2 + 2)
                    if i >= 3 and i % 2:
                        pv((i - 3) // 2)
                    if 1 <= i <= HEADS:
                        turn(i - 1)

            def retrieve(l):
                for i in range(HC):
                    if i >= 4:
                        pe.wait_ge(qryT_ready, HC * l + i - 3)
                    turned_project(PLAN[l]["query"] + i, 0, bank[i % 4][:, 0:S],
                                   ready=(x_lo_ready, NC * (3 * l + 1)) if i == 0 else None)
                pe.wait_ge(qryT_ready, HC * (l + 1))
                pe.wait_ge(layer_loaded, 48 * (l + 1))
                for u in range(2 * 4):
                    t, g = u // 4, u % 4
                    for i in range(4):
                        mm = pe.matmul(bank[4 * (1 - t) + g][:, P * i:P * i + P], qryT[:, 4 * g + i, P * t:P * t + P],
                                       keysT[:, 4 * g + i, :], start=True, stop=True)
                    mm.then_inc(keys_scored, 1)
                pe.wait_ge(key_s_ready, 4 * (l + 1))

            def chunk_u(l, j, k):
                pe.wait_ge(gelu_done, NK * l + k * SLOTS + j + 1)
                turned_project(PLAN[l]["u"] + j, k, bank[4 + j % 2][:, 0:S])

            def chunk_v(l, j, k, first=False, last=False):
                pe.wait_ge(g_hi_ready, NK * l + k * SLOTS + j + 1)
                pe.wait_ge(g_lo_ready, NK * l + k * SLOTS + j + 1)
                multiply(PLAN[l]["v"] + j, k, [(bank[2 * t + b][:, :],
                                                [v[:, j % G_SLOTS, P * t:P * t + P] for v in (g_hi, g_lo)],
                                                slice(512 * b, 512 * b + 512), first, last)
                                               for t in range(NT) for b in range(2)], tile_first=last)

            def gates(l, half, c, k):
                n = S // 4 * (2 * l + half) + c
                pe.wait_ge(hot_ready, n + k * SLOTS + 1)
                pe.wait_ge(gated_done, n + k * SLOTS + 1)
                for q in range(4):
                    for i in range(3):
                        mm = pe.matmul(bank[6 + c % 2][:, J_HALF * q:J_HALF * q + J_HALF], hot_i[:, c % 2, q, :],
                                       hot_jg[:, c % 2, i, q, :], start=i == 0, stop=i == 2)
                mm.then_inc(gates_done, 1)

            def turn_selected(l):
                for t in range(NT):
                    pe.wait_ge(sel_ready, 2 * l + t + 1)
                    for i, e in enumerate((e_i, e_j, e_g)):
                        mm = pe.transpose(bank[6 + t][:, P * i:P * i + P],
                                          e[:, t, :, :].rearrange("p g k -> p (g k)"), ident[:])
                    mm.then_inc(sel_turned, 1)

            def experts(l):
                def chunks_u(first, n):
                    with pe.Fori(0, n // SLOTS) as k:
                        for c in range(SLOTS):
                            chunk_u(l, first + c, k)

                quarter = J_HALF // SLOTS
                chunks_u(0, J_TURN)
                turn_selected(l)
                chunks_u(J_TURN, J_HALF - J_TURN)
                with pe.Fori(0, quarter) as k:
                    for c in range(SLOTS):
                        gates(l, 0, c, k)
                        chunk_u(l, J_HALF + c, k)
                for c in range(SLOTS):
                    gates(l, 1, c, 0)
                    chunk_v(l, c, 0, first=c == 0)
                with pe.Fori(1, quarter) as k:
                    for c in range(SLOTS):
                        gates(l, 1, c, k)
                        chunk_v(l, c, k)
                with pe.Fori(0, quarter - 1) as k:
                    for c in range(SLOTS):
                        chunk_v(l, J_HALF + c, k)
                for c in range(SLOTS):
                    chunk_v(l, NK - SLOTS + c, 0, last=c == SLOTS - 1)

            def embed(l):
                for q in range(4):
                    m = PLAN[l]["up"] + q
                    pe.wait_ge(lo_ready, m + 1 + SLOTS)
                    multiply(m, 0, [(bank[4 + 2 * (q // 2) + t][:, S * (q % 2):S * (q % 2) + S],
                                     [v[:, 512 * c + P * t:512 * c + P * t + P]
                                      for v in (w_hi[:, m % SLOTS, :], w_lo[:, m % LO_SLOTS, :])],
                                     slice(512 * c + S, 512 * c + 2 * S), c == 0, c == 1)
                                    for t in range(NT) for c in range(2)])

            for l in range(LAYERS):
                turn_normed(3 * l)
                project_in(l)
                heads(l)
                for i in range(2):
                    project(PLAN[l]["out"] + 4 * i, i, tile_first=True,
                            ready=(o_lo_ready, PAIRS * l) if i == 0 else None)
                turn_normed(3 * l + 1)
                retrieve(l)
                experts(l)
                embed(l)
                turn_normed(3 * l + 2)
                for i in range(2):
                    project(PLAN[l]["gate"] + 4 * i, i, least=4, tile_first=True,
                            ready=(x_lo_ready, NC * (3 * l + 2)) if i == 0 else None)

        @block.scalar
        def _(act):
            act.sem_inc(hi_ready, SLOTS)
            act.sem_inc(gelu_done, 2)
            split = [0]

            def split_hi(c, k=0):
                act.wait_ge(piece_loaded[c % SLOTS], (k + c // SLOTS + 1) * 16)
                act.wait_ge(piece_used, k * SLOTS + c + 1)
                act.activation(w_hi[:, c % SLOTS, :], raw[:, c % SLOTS, :], ACT.Copy).then_inc(hi_ready, 1)

            def split_to(m):
                while split[0] <= min(m, PIECES - 1):
                    split_hi(split[0])
                    split[0] += 1

            def multiplied(c, k=0):
                act.wait_ge(piece_used, k * SLOTS + c + 1 + SLOTS)

            act.wait_ge(ident_loaded, 32)

            def rope_tables():
                act.wait_ge(angle_ready, 1)
                act.activation(rope_sin[:, :, HALF:ROT], rope_a[:, 0, :, :], ACT.Sin)
                act.activation(rope_cos[:, :, 0:HALF], rope_a[:, 1, :, :], ACT.Sin).then_inc(rope_ready, 1)

            def fetch_roots(n):
                act.activation(table_load[:, n:n + 1], ident[:, 0:1], ACT.Sqrt)

            def square(n, blocks):
                for u in blocks:
                    t, b = BLOCKS[n % 3][u]
                    if n:
                        act.wait_ge(h_written, 4 * (n - 1) + u + 1)
                    else:
                        act.wait_ge(h_loaded[t], 16)
                    act.activation(xs[:, t, 512 * b:512 * b + 512], h[:, t, 512 * b:512 * b + 512], ACT.Square,
                                   accum_out=sumsq[:, t, b:b + 1]).then_inc(sumsq_done, 1)

            def norm(n, ahead=None, squared=0):
                square(n, range(squared, 2 * NT))
                act.wait_ge(var_ready, n + 1)
                act.activation(rstd[:], inv_var[:], ACT.Sqrt).then_inc(rstd_ready, 1)
                if ahead:
                    split_to(ahead)
                for c in range(NC):
                    act.wait_ge(xs_turned, 4 * n + c // 2 + 1)
                    act.activation(x_hi[:, c, :], bank[TURN_BANK[n % 3] + c // 2][:, S * (c % 2):S * (c % 2) + S], ACT.Copy,
                                   scale=gain[:, n * NC + c:n * NC + c + 1]).then_inc(x_hi_ready, 1)

            def take_block(m, i, w, dst, func, between=None, tile=None):
                split_to(m + 1 + AHEAD)
                if between:
                    between()
                split_to(m + 3 + AHEAD)
                for t in range(NT):
                    if tile and t == 0:
                        act.wait_ge(tile_done, tile)
                    else:
                        multiplied(m + 3)
                    act.activation(dst(t), bank[2 * (i % 2) + t][:, 0:w], func).then_inc(proj_taken, 1)

            def square_run(l, r):
                for t in range(NT):
                    x = QK_RUN[l][r]
                    act.activation(squares[:, 2 * r + t, :, :].rearrange("p n d -> p (n d)"), qkv[:, t, x:x + HEADS * DH],
                                   ACT.Square).then_inc(qk_squared, 1)

            def root_run(l, r):
                act.wait_ge(h_var_ready, 2 * l + r + 1)
                act.activation(h_rstd[:, 2 * r:2 * r + 2, :], h_inv_var[:, 2 * r:2 * r + 2, :], ACT.Sqrt).then_inc(h_rstd_ready, 1)

            def heads(l):
                def exps(i):
                    act.wait_ge(negmax_ready, 2 * (HEADS * l + i + 1))
                    if i >= 2:
                        act.wait_ge(probs_ready, 2 * (HEADS * l + i - 1))
                    for t, (x, y) in enumerate(SEG):
                        act.activation(probs[:, i % 2, x:y], biased[:, i % 2, x:y], ACT.Exp,
                                       bias=neg_max[:, i % 2, t:t + 1],
                                       accum_out=denom[:, i % 2, t:t + 1]).then_inc(exp_done, 1)

                def take_probs(i):
                    act.wait_ge(probs_turned, HEADS * l + i + 1)
                    if i >= 4:
                        act.wait_ge(pv_done, PAIRS * l + i // 2 - 1)
                    act.activation(probs_T[:, i % 4, :], bank[2 + i % 2][:, 0:KEYS], ACT.Copy).then_inc(probsT_ready, 1)

                def take_o(p):
                    act.wait_ge(pv_done, PAIRS * l + p + 1)
                    act.activation(x_hi[:, p, :], bank[6 + p % 2][:, 0:S], ACT.Copy).then_inc(o_hi_ready, 1)

                def take_qk(p):
                    act.wait_ge(qk_turned, PAIRS * l + p + 1)
                    act.activation(qkT[:, p, :, :].rearrange("p k t -> p (k t)"), bank[4 + p % 2][:, :],
                                   ACT.Copy).then_inc(qkT_ready, 1)

                take_qk(0)
                take_qk(1)
                for i in range(HEADS + 2):
                    if i < HEADS:
                        exps(i)
                    if i % 2 == 0 and i // 2 + 2 < PAIRS:
                        take_qk(i // 2 + 2)
                    if 1 <= i <= HEADS:
                        take_probs(i - 1)
                    if i >= 3 and i % 2:
                        take_o((i - 3) // 2)

            for l in range(LAYERS):
                plan = PLAN[l]
                fetch_roots(3 * l)
                if l:
                    split_to(plan["in"] + AHEAD - 1)
                norm(3 * l, ahead=plan["in"] + AHEAD - 1, squared=NT if l else 0)
                for dst, name in ((mask_bias, "mask_bias"), (head_gain, "head_gain"), (keysT, "keysT")):
                    act.dma_start(dst, a[name][l]).then_inc(layer_loaded, 16)
                for i, b in enumerate(IN_ORDER[l]):
                    w = min(512, IN_WIDTH[l] - 512 * b)
                    last = i == len(IN_ORDER[l]) - 1
                    take_block(plan["in"] + 4 * i, i, w, lambda t: qkv[:, t, 512 * b:512 * b + w], ACT.Copy,
                               between=(lambda: root_run(l, 1)) if last else rope_tables if l == i == 0 else None)
                    if l == 0 and i == 1:
                        for t in range(NT):
                            act.wait_ge(idx_turned, t + 1)
                            act.activation(idxT[:, :, P * t:P * t + P],
                                           bank[6 + t][:, 0:3 * P].rearrange("p (a t) -> p a t", a=3),
                                           ACT.Copy).then_inc(idxT_ready, 1)
                    if i in (2 - l, 4 - l):
                        act.wait_ge(proj_taken, TAKEN[l] + 2 * (i + 1))
                        square_run(l, (i - 1) // 2)
                    if i == 4 - l:
                        root_run(l, 0)
                heads(l)
                fetch_roots(3 * l + 1)
                split_to(plan["query"] + AHEAD - 1)
                norm(3 * l + 1)
                for i in range(HC):
                    split_to(plan["query"] + i + AHEAD)
                    multiplied(plan["query"] + i)
                    act.activation(qryT[:, i, :], bank[i % 4][:, 0:S], ACT.Copy).then_inc(qryT_ready, 1)
                for g in range(4):
                    act.wait_ge(keys_scored, 8 * l + g + 1)
                    act.activation(key_s[:, 4 * g:4 * g + 4, :].rearrange("p a k -> p (a k)"), bank[4 + g][:, :],
                                   ACT.Copy).then_inc(key_s_ready, 1)

                def gelu(j, k=0):
                    multiplied(plan["u"] + j, k)
                    act.activation(act_ijt[:, bass.ds(k * SLOTS + j, 1), :].rearrange("p a t -> p (a t)"),
                                   bank[4 + j % 2][:, 0:S], ACT.Gelu_apprx_tanh).then_inc(gelu_done, 1)

                def gelus(first, n):
                    with act.Fori(0, n // SLOTS) as k:
                        for c in range(SLOTS):
                            gelu(first + c, k)
                            split_hi(plan["u"] + first + c + AHEAD, k)
                    split[0] += n

                gelus(0, J_EXP)
                for t in range(NT):
                    act.wait_ge(cand_ready, 2 * l + t + 1)
                    act.activation(e_g[:, t, :, :], cv[:, t, :, :], ACT.Exp).then_inc(gexp_done, 1)
                gelus(J_EXP, J_HALF - J_EXP)
                act.wait_ge(sel_turned, 2 * (l + 1))
                gelus(J_HALF, J_HALF - SLOTS)
                for j in range(NK - SLOTS, NK):
                    gelu(j)
                    if j < NK - 1:
                        split_to(plan["u"] + j + AHEAD)

                def take_gated(j, k=0):
                    multiplied(plan["v"] + j - G_SLOTS, k)
                    act.activation(g_hi[:, j % G_SLOTS, :], act_ijt[:, bass.ds(k * SLOTS + j, 1), :]
                                   .rearrange("p a t -> p (a t)"), ACT.Copy).then_inc(g_hi_ready, 1)

                for half in range(2):
                    act.wait_ge(gated_done, S // 4 * (2 * l + half + 1) + 2)
                    take_gated(J_HALF * half)
                    take_gated(J_HALF * half + 1)
                    split_to(plan["v"] + AHEAD - 1)
                    with act.Fori(0, J_HALF // SLOTS - 1) as k:
                        for c in range(SLOTS):
                            split_hi(plan["v"] + J_HALF * half + c + AHEAD, k)
                            take_gated(J_HALF * half + c + 2, k)
                    for c in range(J_HALF - SLOTS, J_HALF):
                        split_hi(plan["v"] + J_HALF * half + c + AHEAD)
                        if c + 2 < J_HALF:
                            take_gated(J_HALF * half + c + 2)
                    split[0] += J_HALF
                fetch_roots(3 * l + 2)
                split_to(plan["up"] + 3)
                norm(3 * l + 2, ahead=plan["gate"] + 1)
                for i in range(2):
                    take_block(plan["gate"] + 4 * i, i, 512, lambda t: sig[:, t, 512 * i:512 * i + 512], ACT.Sigmoid,
                               between=(lambda: square(3 * l + 3, range(NT))) if i and l < LAYERS - 1 else None,
                               tile=5 * l + 4 + i)

        @block.vector
        def _(dve):
            steps = [0]

            def link(ins):
                steps[0] += 1
                ins.then_inc(dve_step, 1)
                dve.wait_ge(dve_step, steps[0])

            def multiplied(c):
                dve.wait_ge(piece_used, c + 1 + SLOTS)

            dve.sem_inc(gated_done, 2)
            dve.wait_ge(ident_loaded, 32)
            dve.wait_ge(const_loaded, 16 * CONSTS)
            link(dve.tensor_copy(iota_bf[:], iota[:]))

            def rope_tables():
                link(dve.tensor_copy(pos_f[:], pos_i[:]))
                for t in range(NT):
                    ins = dve.tensor_scalar(rope_a[:, 2, t, :], inv_freq[:], pos_f[:, t:t + 1], None, ALU.mult)
                link(ins)
                for i in range(2):
                    src = rope_a[:, 2, :, :]
                    link(dve.tensor_scalar(rope_a[:, 3, :, :], src, 1.0 / (2 * np.pi), 0.25 * i, ALU.mult, ALU.add))
                    link(dve.tensor_scalar(rope_a[:, 3, :, :], rope_a[:, 3, :, :], ROUND, -ROUND, ALU.add, ALU.add))
                    for part in TWO_PI_PARTS:
                        link(dve.scalar_tensor_tensor(rope_a[:, i, :, :], rope_a[:, 3, :, :], -part, src, ALU.mult, ALU.add))
                        src = rope_a[:, i, :, :]
                    if i:
                        link(dve.tensor_scalar(src, src, np.pi / 2, None, ALU.add))
                    link(dve.tensor_scalar(src, src, 3.1415925, -3.1415925, ALU.min, ALU.max))
                dve.sem_inc(angle_ready, 1)
                dve.wait_ge(rope_ready, 1)
                dve.tensor_scalar(rope_sin[:, :, 0:HALF], rope_sin[:, :, HALF:ROT], -1.0, None, ALU.mult)
                link(dve.tensor_copy(rope_cos[:, :, HALF:ROT], rope_cos[:, :, 0:HALF]))

            def norm(n):
                dve.wait_ge(sumsq_done, 4 * (n + 1))
                link(dve.tensor_tensor(mean_sq[:], sumsq[:, :, 0], sumsq[:, :, 1], ALU.add))
                link(dve.tensor_scalar(mean_sq[:], mean_sq[:], 1.0 / D, EPS, ALU.mult, ALU.add))
                dve.reciprocal(inv_var[:], mean_sq[:]).then_inc(var_ready, 1)
                dve.wait_ge(rstd_ready, n + 1)
                for t in range(NT):
                    for b in range(2):
                        cols = slice(512 * b, 512 * b + 512)
                        dve.tensor_scalar(xs[:, t, cols], h[:, t, cols], rstd[:, t:t + 1], None,
                                          ALU.mult).then_inc(xs_ready, 1)
                for c in range(NC):
                    dve.wait_ge(x_hi_ready, NC * n + 2 * (c // 2) + 2)
                    dve.scalar_tensor_tensor(x_lo[:, c, :], bank[TURN_BANK[n % 3] + c // 2][:, S * (c % 2):S * (c % 2) + S],
                                             gain[:, n * NC + c:n * NC + c + 1], x_hi_f[:, c, :], ALU.mult,
                                             ALU.subtract).then_inc(x_lo_ready, 1)

            def rope(x, n, t):
                def table(v):
                    return v.unsqueeze(1).broadcast_to([P, n, v.shape[-1]])
                dve.tensor_tensor(rope_t[:, 0, 0:n, :], x[:, :, 0:ROT], table(rope_cos[:, t, :]), ALU.mult)
                dve.tensor_tensor(rope_t[:, 1, 0:n, 0:HALF], x[:, :, HALF:ROT], table(rope_sin[:, t, 0:HALF]), ALU.mult)
                link(dve.tensor_tensor(rope_t[:, 1, 0:n, HALF:ROT], x[:, :, 0:HALF], table(rope_sin[:, t, HALF:ROT]), ALU.mult))
                return dve.tensor_tensor(x[:, :, 0:ROT], rope_t[:, 0, 0:n, :], rope_t[:, 1, 0:n, :], ALU.add)

            def var_run(l, r):
                for t in range(NT):
                    u = 2 * r + t
                    dve.wait_ge(qk_squared, 4 * l + u + 1)
                    ins = dve.tensor_reduce(h_sumsq[:, u, :], squares[:, u, :, :], AX_X, ALU.add)
                link(ins)
                v = h_sumsq[:, 2 * r:2 * r + 2, :]
                link(dve.tensor_scalar(v, v, 1.0 / DH, EPS, ALU.mult, ALU.add))
                dve.reciprocal(h_inv_var[:, 2 * r:2 * r + 2, :], v).then_inc(h_var_ready, 1)

            def norm_run(l, r):
                dve.wait_ge(h_rstd_ready, 2 * l + r + 1)
                for t in range(NT):
                    u, c = 2 * r + t, QK_RUN[l][r]
                    x = qkv[:, t, c:c + HEADS * DH].rearrange("p (n d) -> p n d", d=DH)
                    link(dve.tensor_tensor(x, x, h_rstd[:, u, :].unsqueeze(2).broadcast_to([P, HEADS, DH]), ALU.mult))
                    x4 = x.rearrange("p (b n) d -> p b n d", b=2)
                    link(dve.tensor_tensor(x4, x4, head_gain[:, r, :, :].unsqueeze(2).broadcast_to([P, 2, 8, DH]),
                                           ALU.mult))
                    rope(x, HEADS, t).then_inc(qk_ready, 1)

            def rope_indexer():
                dve.wait_ge(proj_taken, NT)
                for t in range(NT):
                    x = qkv[:, t, IDX_COL:WI_COL].rearrange("p (n d) -> p n d", d=DH)
                    link(rope(x, IDX_HEADS + 1, t))
                    dve.tensor_copy(kk[:, t, :].rearrange("p (b d) -> p b d", b=2),
                                    x[:, IDX_HEADS:IDX_HEADS + 1, :].broadcast_to([P, 2, DH])).then_inc(idx_ready, 1)

            def index_scores():
                for t, (x, y) in enumerate(SEG):
                    dve.wait_ge(logits_done, t + 1)
                    for i in range(IDX_HEADS):
                        src = bank[6][:, P * i:P * i + P] if t == 0 else bank[4 + i // 2][:, S * (i % 2):S * (i % 2) + S]
                        dst = idx_r if i else idx_s
                        link(dve.tensor_scalar(dst[:, x:y], src, 0.0, qkv[:, t, WI_COL + i:WI_COL + i + 1], ALU.max, ALU.mult))
                        if i:
                            link(dve.tensor_tensor(idx_s[:, x:y], idx_s[:, x:y], idx_r[:, x:y], ALU.add))
                dve.tensor_tensor(idx_s[:], idx_s[:], mask_bias[:], ALU.add).then_inc(logits_taken, 1)
                dve.wait_ge(logits_taken, 1)

            def select_dsa(t):
                x, y = SEG[t]
                for _ in range(DSA_TOPK // 8):
                    link(dve.max(out=top8[:], in_=idx_s[:, x:y]))
                    link(dve.match_replace(out=idx_s[:, x:y], in_to_replace=top8[:], in_values=idx_s[:, x:y], imm_value=GONE))
                link(dve.tensor_scalar(idx_r[:, x:y], idx_s[:, x:y], GONE / 2, NEG, ALU.is_gt, ALU.mult))
                link(dve.tensor_tensor(bias_dsa[:, x:y], idx_r[:, x:y], mask_bias[:, x:y], ALU.add))

            def heads(l):
                def bias(i):
                    mask = bias_dsa if l == 0 and i >= 8 else mask_bias
                    dve.wait_ge(scores_done, HEADS * l + i + 1)
                    if i >= 2:
                        dve.wait_ge(exp_done, 2 * (HEADS * l + i - 1))
                    dve.scalar_tensor_tensor(biased[:, i % 2, :], bank[i % 2][:, 0:KEYS], SCALE, mask[:, :], ALU.mult,
                                             ALU.add).then_inc(biased_ready, 1)
                    dve.wait_ge(biased_ready, HEADS * l + i + 1)
                    for t, (x, y) in enumerate(SEG):
                        dve.tensor_reduce(neg_max[:, i % 2, t:t + 1], biased[:, i % 2, x:y], AX_X, ALU.max,
                                          negate=True).then_inc(negmax_ready, 1)

                def scale(i):
                    dve.wait_ge(exp_done, 2 * (HEADS * l + i + 1))
                    if i >= 2:
                        dve.wait_ge(probs_turned, HEADS * l + i - 1)
                    link(dve.reciprocal(inv_denom[:, i % 2, :], denom[:, i % 2, :]))
                    for t, (x, y) in enumerate(SEG):
                        dve.tensor_scalar(probs_n[:, i % 2, x:y], probs[:, i % 2, x:y], inv_denom[:, i % 2, t:t + 1], None,
                                          ALU.mult).then_inc(probs_ready, 1)

                def take_o(p):
                    dve.wait_ge(o_hi_ready, PAIRS * l + p + 1)
                    dve.tensor_tensor(x_lo[:, p, :], bank[6 + p % 2][:, 0:S], x_hi_f[:, p, :], ALU.subtract).then_inc(o_lo_ready, 1)

                for i in range(HEADS + 3):
                    if i < HEADS:
                        bias(i)
                    if 1 <= i <= HEADS:
                        scale(i - 1)
                    if i >= 4 and i % 2 == 0:
                        take_o((i - 4) // 2)

            def add_out(l):
                for t, b in BLOCKS[1]:
                    if t == 0:
                        dve.wait_ge(tile_done, 5 * l + b + 1)
                    else:
                        multiplied(PLAN[l]["out"] + 4 * b + 3)
                    x = h[:, t, 512 * b:512 * b + 512]
                    dve.tensor_tensor(x, x, bank[2 * b + t][:, :], ALU.add).then_inc(h_written, 1)

            def add_experts(l):
                for t, b in BLOCKS[2]:
                    if t == 0:
                        dve.wait_ge(tile_done, 5 * l + 3)
                    else:
                        multiplied(PLAN[l]["v"] + NK - 1)
                    x = h[:, t, 512 * b:512 * b + 512]
                    dve.tensor_tensor(x, x, bank[2 * t + b][:, :], ALU.add).then_inc(h_written, 1)

            def add_embedding(l):
                for u, (t, b) in enumerate(BLOCKS[0]):
                    dve.wait_ge(proj_taken, TAKEN[l] + 2 * len(IN_ORDER[l]) + u + 1)
                    x, gate = (v[:, t, 512 * b:512 * b + 512] for v in (h, sig))
                    link(dve.tensor_tensor(gate, gate, bank[4 + 2 * b + t][:, :], ALU.mult))
                    dve.tensor_tensor(x, x, gate, ALU.add).then_inc(h_written, 1)

            def top16(values, indices, src):
                link(dve.max(out=values[:, 0:8], in_=src))
                dve.max_index(out=indices[:, 0:8], in_max=values[:, 0:8], in_values=src)
                link(dve.match_replace(out=src, in_to_replace=values[:, 0:8], in_values=src, imm_value=GONE))
                link(dve.max(out=values[:, 8:16], in_=src))
                return dve.max_index(out=indices[:, 8:16], in_max=values[:, 8:16], in_values=src)

            def select_experts(l):
                for t in range(NT):
                    for n in range(HC):
                        if t == 0:
                            dve.wait_ge(key_s_ready, 4 * l + n // 4 + 1)
                            src = key_s[:, n, :]
                        else:
                            dve.wait_ge(keys_scored, 8 * l + 4 + n // 4 + 1)
                            src = bank[n // 4][:, NK * (n % 4):NK * (n % 4) + NK]
                        ins = top16(sv[:, n, :], si[:, n, :], src)
                    link(ins)
                    halves = sv[:, :, :].rearrange("p (g c) k -> p g c k", c=2)
                    link(dve.tensor_tensor(cand, halves[:, :, 0, :].unsqueeze(3).broadcast_to([P, PH, TOPK, TOPK]),
                                           halves[:, :, 1, :].unsqueeze(2).broadcast_to([P, PH, TOPK, TOPK]), ALU.add))
                    dve.tensor_copy(si_f, si)
                    for g in range(PH):
                        ins = top16(cv[:, t, g, :], ci[:, g, :], cand[:, g, :, :].rearrange("p a b -> p (a b)"))
                    link(ins)
                    dve.tensor_scalar(rank[:, 0, :, :], ci, 4, None, ALU.logical_shift_right)
                    link(dve.tensor_scalar(rank[:, 1, :, :], ci, 15, None, ALU.bitwise_and))
                    link(dve.tensor_copy(rank_f, rank))
                    idx = si_f[:, :, :].rearrange("p (g c) k -> p g c k", c=2)
                    for c, e in enumerate((e_i, e_j)):
                        link(dve.tensor_tensor(eq, rank_f[:, c, :, :].unsqueeze(3).broadcast_to([P, PH, TOPK, TOPK]),
                                               iota[:, 0:TOPK].unsqueeze(1).unsqueeze(1).broadcast_to([P, PH, TOPK, TOPK]),
                                               ALU.is_equal))
                        link(dve.tensor_tensor(eq, eq, idx[:, :, c, :].unsqueeze(2).broadcast_to([P, PH, TOPK, TOPK]), ALU.mult))
                        link(dve.tensor_reduce(e[:, t, :, :], eq, AX_X, ALU.add))
                    link(dve.tensor_reduce(g_inv[:, t, :], cv[:, t, :, :], AX_X, ALU.max))
                    dve.tensor_tensor(cv[:, t, :, :], cv[:, t, :, :], g_inv[:, t, :].unsqueeze(2).broadcast_to([P, PH, TOPK]),
                                      ALU.subtract).then_inc(cand_ready, 1)
                for t in range(NT):
                    dve.wait_ge(gexp_done, 2 * l + t + 1)
                    link(dve.tensor_reduce(g_sum[:, t, :], e_g[:, t, :, :], AX_X, ALU.add))
                    link(dve.reciprocal(g_inv[:, t, :], g_sum[:, t, :]))
                    dve.tensor_tensor(e_g[:, t, :, :], e_g[:, t, :, :], g_inv[:, t, :].unsqueeze(2).broadcast_to([P, PH, TOPK]),
                                      ALU.mult).then_inc(sel_ready, 1)
                for t in range(NT):
                    dve.wait_ge(sel_turned, 2 * l + t + 1)
                    tok = slice(P * t, P * t + P)
                    dve.tensor_copy(ijT[:, :, tok], bank[6 + t][:, 0:2 * P].rearrange("p (e t) -> p e t", e=2))
                    src = bank[6 + t][:, 2 * P:3 * P]
                    link(dve.tensor_copy(gT[:, 0, tok], src))
                    for i in range(2):
                        link(dve.tensor_tensor(g_rest[:, i, tok], src, gT[:, i, tok], ALU.subtract))
                        src = g_rest[:, i, tok]
                        link(dve.tensor_copy(gT[:, i + 1, tok], src))

            def hot(l, half, c, k):
                n = S // 4 * (2 * l + half) + c
                dve.wait_ge(gates_done, n + k * SLOTS + 1)
                tok = bass.ds(k * (4 * SLOTS) + 4 * c, 4)
                dve.tensor_tensor(hot_j[:, c % 2, :, :], iota_bf[:, J_HALF * half:J_HALF * half + J_HALF].unsqueeze(1)
                                  .broadcast_to([P, 4, J_HALF]), ijT[:, 1, tok].unsqueeze(2).broadcast_to([P, 4, J_HALF]),
                                  ALU.is_equal).then_inc(hot_j_ready, 1)
                dve.tensor_tensor(hot_i[:, c % 2, :, :], iota_bf[:, :].unsqueeze(1).broadcast_to([P, 4, P]),
                                  ijT[:, 0, tok].unsqueeze(2).broadcast_to([P, 4, P]), ALU.is_equal)
                dve.wait_ge(hot_j_ready, n + k * SLOTS + 1)
                dve.tensor_tensor(hot_jg[:, c % 2, :, :, :], hot_j[:, c % 2, :, :].unsqueeze(1).broadcast_to([P, 3, 4, J_HALF]),
                                  gT[:, :, tok].unsqueeze(3).broadcast_to([P, 3, 4, J_HALF]), ALU.mult).then_inc(hot_ready, 1)

            def gated(l, half, c, k):
                n = S // 4 * (2 * l + half) + c
                tok = bass.ds(k * (4 * SLOTS) + 4 * c, 4)
                dve.wait_ge(gates_done, n + k * SLOTS + 3)
                x = act_itj[:, tok, J_HALF * half:J_HALF * half + J_HALF]
                dve.tensor_tensor(x, x, bank[6 + c % 2][:, 0:4 * J_HALF].rearrange("p (q j) -> p q j", q=4),
                                  ALU.mult).then_inc(gated_done, 1)

            def gated_lo(l, j, k):
                dve.wait_ge(g_hi_ready, NK * l + k * SLOTS + j + 1)
                dve.tensor_tensor(g_lo[:, j % G_SLOTS, :], act_ijt[:, bass.ds(k * SLOTS + j, 1), :].rearrange("p a t -> p (a t)"),
                                  g_hi_f[:, j % G_SLOTS, :], ALU.subtract).then_inc(g_lo_ready, 1)

            def gate_experts(l):
                quarter = J_HALF // SLOTS
                hot(l, 0, 0, 0)
                dve.wait_ge(gelu_done, NK * l + J_HALF + 2)
                for c in range(1, SLOTS):
                    hot(l, 0, c, 0)
                    gated(l, 0, c - 1, 0)
                with dve.Fori(1, quarter) as k:
                    for c in range(SLOTS):
                        hot(l, 0, c, k)
                        gated(l, 0, c - 1, k)
                gated(l, 0, J_HALF - 1, 0)
                hot(l, 1, 0, 0)
                dve.wait_ge(gelu_done, NK * (l + 1) + 2)
                gated_lo(l, 0, 0)
                for c in range(1, SLOTS):
                    hot(l, 1, c, 0)
                    gated_lo(l, c, 0)
                    gated(l, 1, c - 1, 0)
                with dve.Fori(1, quarter) as k:
                    for c in range(SLOTS):
                        hot(l, 1, c, k)
                        gated_lo(l, c, k)
                        gated(l, 1, c - 1, k)
                gated(l, 1, J_HALF - 1, 0)
                with dve.Fori(0, quarter) as k:
                    for c in range(SLOTS):
                        gated_lo(l, J_HALF + c, k)

            for l in range(LAYERS):
                norm(3 * l)
                if l == 0:
                    rope_tables()
                    rope_indexer()
                dve.wait_ge(layer_loaded, 48 * (l + 1))
                if l == 0:
                    index_scores()
                    select_dsa(0)
                    var_run(l, 0)
                    select_dsa(1)
                else:
                    var_run(l, 0)
                norm_run(l, 0)
                var_run(l, 1)
                norm_run(l, 1)
                heads(l)
                add_out(l)
                norm(3 * l + 1)
                select_experts(l)
                gate_experts(l)
                add_experts(l)
                norm(3 * l + 2)
                add_embedding(l)


def by_blocks(w, order):
    for b in order:
        block = w[:, 512 * b:512 * b + 512]
        yield np.pad(block, ((0, 0), (0, 512 - block.shape[1]))).reshape(4, 2, P, 512).transpose(0, 2, 1, 3)


def by_columns(w):
    return w.reshape(NC, P, -1, P).transpose(2, 1, 0, 3)


def weight_stream(i):
    stream = np.empty((PIECES, P, PIECE), np.float32)
    at = 0

    def put(pieces):
        nonlocal at
        n = len(pieces)
        stream[at:at + n].reshape((n, *pieces.shape[1:]))[...] = pieces
        at += n

    for l, (w_in, w_out) in enumerate((("ab_w_in", "ab_w_out"), ("c_w_in", "c_w_out"))):
        for pieces in by_blocks(i[w_in][0], IN_ORDER[l]):
            put(pieces)
        for pieces in by_blocks(i[w_out][0], range(2)):
            put(pieces)
        put(by_columns(i["peer_w_query"][l]))
        put(i["peer_u"][l].reshape(NK, NK, NC, P).transpose(1, 3, 2, 0))
        put(i["peer_v"][l].reshape(NK, NK, D).transpose(1, 0, 2))
        emb = i["p"][l, 0].T.reshape(2, P, S).transpose(1, 0, 2)
        up = i["ple_w_up"][l].reshape(2, P, 4, S).transpose(2, 1, 0, 3)
        put(np.stack([np.concatenate([emb, u], axis=2) for u in up]))
        for pieces in by_blocks(i["ple_w_gate"][l], range(2)):
            put(pieces)
    assert at == PIECES
    return stream


def shape_constants():
    t = np.arange(P)[:, None]
    causal, dilated = [], []
    for tile, (x, y) in enumerate(SEG):
        dist = t + P * tile - np.arange(y - x)[None, :]
        count = np.zeros(dist.shape, np.int64)
        for window, dil in ((128, 1), (512, 4), (2048, 16)):
            count += (dist >= 0) & (dist <= window) & (dist % dil == 0)
        causal.append(np.where(dist >= 0, 0.0, NEG))
        dilated.append(np.where(count > 0, np.log(np.maximum(count, 1)), NEG))
    half = np.arange(HALF, dtype=np.float32)
    inv = np.power(np.float32(500000.0), -half / np.float32(HALF)).astype(np.float32)
    return {
        "ident": np.eye(P, dtype=np.float32),
        "iota": np.tile(np.arange(P, dtype=np.float32), (P, 1)),
        "mask_bias": np.stack([np.concatenate(v, axis=1) for v in (causal, dilated)]).astype(np.float32),
        "inv_freq": np.tile(inv, (P, 1)),
    }


def lay_out(i):
    a = shape_constants()
    c = np.ascontiguousarray
    a["x"] = c(i["x"][0])
    a["positions"] = c(i["positions"][0].reshape(NT, P).T)
    gains = np.stack([i[n][l] for l in range(LAYERS) for n in ("attn_norm", "ffn_norm", "ple_norm")])
    a["gain"] = c(gains.reshape(3 * LAYERS * NC, P).T)
    hg = np.stack([i["a_q_norm"][0], i["a_k_norm"][0], i["b_q_norm"][0], i["b_k_norm"][0],
                   i["c_q_norm"][0], i["c_q_norm"][0], i["c_k_norm"][0], i["c_k_norm"][0]])
    a["head_gain"] = c(np.broadcast_to(hg.reshape(LAYERS, 1, 2, 2, DH), (LAYERS, P, 2, 2, DH)))
    a["keysT"] = c(i["peer_sub_keys"].reshape(LAYERS, HC, NK, P).transpose(0, 3, 1, 2))
    a["stream"] = weight_stream(i)
    return a


def kernel(**inputs):
    import concourse.bacc as bacc
    from concourse.bass_utils import run_bass_kernel_spmd

    arrays = lay_out({k: np.asarray(v) for k, v in inputs.items()})
    nc = bacc.Bacc("TRN2", target_bir_lowering=False, num_devices=1)
    aps = {k: nc.dram_tensor(f"in_{k}", v.shape, mybir.dt.from_np(v.dtype), kind="ExternalInput").ap()
           for k, v in arrays.items()}
    out = nc.dram_tensor("out", (S, D), F32, kind="ExternalOutput").ap()
    hybrid_trunk(nc, aps, out)
    r = run_bass_kernel_spmd(nc, [{f"in_{k}": v for k, v in arrays.items()}], core_ids=[0])
    return r.results[0]["out"].reshape(1, S, D)
```
